# Optimizing a Trainium2 kernel written in Bass

```python
import math
import jax, jax.numpy as jnp
from jax import lax
import numpy as np

D_MODEL = 2048
BATCH = 1
SEQ = 256
DEPTH = 2

N_A = DEPTH // 2
N_B = DEPTH - N_A
DIFF_HEADS = 16
DIFF_HEAD_DIM = D_MODEL // DIFF_HEADS // 2
DIFF_V_DIM = 2 * DIFF_HEAD_DIM
SB_HEADS = 16
SB_HEAD_DIM = D_MODEL // SB_HEADS
D_FF = -(-8 * D_MODEL // (3 * 256)) * 256
N_BUCKETS = 32
MAX_DISTANCE = 128
Q_BLOCK = 128
RMS_EPS = 1e-5

kernel_name = "yoco_diff_stickbreaking_trunk"

def rmsnorm(x, g):
    xf = x.astype(jnp.float32)
    y = xf * lax.rsqrt(jnp.mean(xf * xf, axis=-1, keepdims=True) + RMS_EPS)
    return (y * g.astype(jnp.float32)).astype(x.dtype)

def t5_bucket(rel):
    max_exact = N_BUCKETS // 2
    n = jnp.maximum(rel, 0)
    nf = jnp.maximum(n, 1).astype(jnp.float32)
    large = max_exact + (jnp.log(nf / max_exact) / math.log(MAX_DISTANCE / max_exact)
                         * (N_BUCKETS - max_exact)).astype(jnp.int32)
    large = jnp.minimum(large, N_BUCKETS - 1)
    return jnp.where(n < max_exact, n, large)

def lambda_init_fn(layer):
    return 0.8 - 0.6 * math.exp(-0.3 * layer)

def diff_attention(h, w_qkv, w_o, lq1, lk1, lq2, lk2, subln_g, rel_bias, lambda_init):
    B, S, _ = h.shape
    H, dh, dv = DIFF_HEADS, DIFF_HEAD_DIM, DIFF_V_DIM
    nb = S // Q_BLOCK
    qkv = h @ w_qkv
    q, k, v = jnp.split(qkv, 3, axis=-1)
    q = q.reshape(B, S, 2 * H, dh).transpose(0, 2, 1, 3) * (dh ** -0.5)
    k = k.reshape(B, S, 2 * H, dh).transpose(0, 2, 1, 3)
    v = v.reshape(B, S, H, dv).transpose(0, 2, 1, 3)
    lam = (jnp.exp(jnp.sum(lq1.astype(jnp.float32) * lk1.astype(jnp.float32)))
           - jnp.exp(jnp.sum(lq2.astype(jnp.float32) * lk2.astype(jnp.float32)))
           + lambda_init)
    k_pos = jnp.arange(S)
    qb = q.reshape(B, 2 * H, nb, Q_BLOCK, dh).transpose(2, 0, 1, 3, 4)

    def block(args):
        qi, i = args
        q_pos = i * Q_BLOCK + jnp.arange(Q_BLOCK)
        rel = q_pos[:, None] - k_pos[None, :]
        bias = jnp.transpose(rel_bias[t5_bucket(rel)], (2, 0, 1)).astype(jnp.float32)
        s = jnp.einsum('bhqd,bhkd->bhqk', qi, k).astype(jnp.float32)
        s = s.reshape(B, H, 2, Q_BLOCK, S) + bias[None, :, None]
        s = jnp.where(rel >= 0, s, -jnp.inf)
        p = jax.nn.softmax(s, axis=-1)
        a = p[:, :, 0] - lam * p[:, :, 1]
        return jnp.einsum('bhqk,bhkd->bhqd', a.astype(v.dtype), v)

    o = lax.map(block, (qb, jnp.arange(nb)))
    o = o.transpose(1, 2, 0, 3, 4).reshape(B, H, S, dv)
    o = rmsnorm(o, subln_g) * (1.0 - lambda_init)
    o = o.transpose(0, 2, 1, 3).reshape(B, S, H * dv)
    return o @ w_o

def shared_kv(h, kv_norm_g, w_kv):
    B, S, _ = h.shape
    kv = rmsnorm(h, kv_norm_g) @ w_kv
    k, v = jnp.split(kv, 2, axis=-1)
    k = k.reshape(B, S, SB_HEADS, SB_HEAD_DIM).transpose(0, 2, 1, 3)
    v = v.reshape(B, S, SB_HEADS, SB_HEAD_DIM).transpose(0, 2, 1, 3)
    return k, v

def stick_breaking(h, w_q, w_o, k, v):
    B, S, _ = h.shape
    H, dh = SB_HEADS, SB_HEAD_DIM
    nb = S // Q_BLOCK
    q = (h @ w_q).reshape(B, S, H, dh).transpose(0, 2, 1, 3) * (dh ** -0.5)
    qb = q.reshape(B, H, nb, Q_BLOCK, dh).transpose(2, 0, 1, 3, 4)
    k_pos = jnp.arange(S)

    def block(args):
        qi, i = args
        q_pos = i * Q_BLOCK + jnp.arange(Q_BLOCK)
        causal = k_pos[None, :] < q_pos[:, None]
        z = jnp.einsum('bhqd,bhkd->bhqk', qi, k).astype(jnp.float32)
        log_not = jnp.where(causal, jax.nn.log_sigmoid(-z), 0.0)
        after = lax.cumsum(log_not, axis=log_not.ndim - 1, reverse=True) - log_not
        a = jnp.where(causal, jnp.exp(jax.nn.log_sigmoid(z) + after), 0.0)
        return jnp.einsum('bhqk,bhkd->bhqd', a.astype(v.dtype), v)

    o = lax.map(block, (qb, jnp.arange(nb)))
    o = o.transpose(1, 0, 3, 2, 4).reshape(B, S, H * dh)
    return o @ w_o

def swiglu(h, w_gate, w_up, w_down):
    return (jax.nn.silu(h @ w_gate) * (h @ w_up)) @ w_down

def setup_inputs(seed: int = 0) -> dict:
    key = jax.random.key(seed)
    ks = jax.random.split(key, 20)
    D, F = D_MODEL, D_FF
    f32 = jnp.float32

    def w(k, shape, fan_in):
        return jax.random.normal(k, shape, f32) * (fan_in ** -0.5)

    def gain(k, shape):
        return 1.0 + 0.02 * jax.random.normal(k, shape, f32)

    return {
        "x": jax.random.normal(ks[0], (BATCH, SEQ, D), f32),
        "rel_bias": 0.5 * jax.random.normal(ks[1], (N_BUCKETS, DIFF_HEADS), f32),
        "attn_norm_g": gain(ks[2], (DEPTH, D)),
        "ffn_norm_g": gain(ks[3], (DEPTH, D)),
        "diff_w_qkv": w(ks[4], (N_A, D, 3 * D), D),
        "diff_w_o": w(ks[5], (N_A, D, D), D),
        "diff_lambda_q1": 0.1 * jax.random.normal(ks[6], (N_A, DIFF_HEAD_DIM), f32),
        "diff_lambda_k1": 0.1 * jax.random.normal(ks[7], (N_A, DIFF_HEAD_DIM), f32),
        "diff_lambda_q2": 0.1 * jax.random.normal(ks[8], (N_A, DIFF_HEAD_DIM), f32),
        "diff_lambda_k2": 0.1 * jax.random.normal(ks[9], (N_A, DIFF_HEAD_DIM), f32),
        "diff_subln_g": gain(ks[10], (N_A, DIFF_V_DIM)),
        "kv_norm_g": gain(ks[11], (D,)),
        "sb_w_kv": w(ks[12], (D, 2 * D), D),
        "sb_w_q": w(ks[13], (N_B, D, D), D),
        "sb_w_o": w(ks[14], (N_B, D, D), D),
        "ffn_w_gate": w(ks[15], (DEPTH, D, F), D),
        "ffn_w_up": w(ks[16], (DEPTH, D, F), D),
        "ffn_w_down": w(ks[17], (DEPTH, F, D), F),
        "final_norm_g": gain(ks[18], (D,)),
    }

def reference(x, rel_bias, attn_norm_g, ffn_norm_g, diff_w_qkv, diff_w_o,
              diff_lambda_q1, diff_lambda_k1, diff_lambda_q2, diff_lambda_k2,
              diff_subln_g, kv_norm_g, sb_w_kv, sb_w_q, sb_w_o,
              ffn_w_gate, ffn_w_up, ffn_w_down, final_norm_g):
    h = x
    k_sh = v_sh = None
    for l in range(DEPTH):
        if l == N_A:
            k_sh, v_sh = shared_kv(h, kv_norm_g, sb_w_kv)
        hn = rmsnorm(h, attn_norm_g[l])
        if l < N_A:
            mix = diff_attention(hn, diff_w_qkv[l], diff_w_o[l],
                                 diff_lambda_q1[l], diff_lambda_k1[l],
                                 diff_lambda_q2[l], diff_lambda_k2[l],
                                 diff_subln_g[l], rel_bias, lambda_init_fn(l))
        else:
            j = l - N_A
            mix = stick_breaking(hn, sb_w_q[j], sb_w_o[j], k_sh, v_sh)
        h = h + mix
        h = h + swiglu(rmsnorm(h, ffn_norm_g[l]), ffn_w_gate[l], ffn_w_up[l], ffn_w_down[l])
    return rmsnorm(h, final_norm_g)


_drawn_inputs = setup_inputs


def setup_inputs(seed=0):
    import zlib

    import numpy as np

    out = dict(_drawn_inputs(seed))
    spreads = {}
    factors = {'ffn_norm_g': 3.427,
     'diff_lambda_q1': 2.866,
     'diff_lambda_k2': 8.0,
     'diff_subln_g': 3.328,
     'kv_norm_g': 18.65,
     'final_norm_g': 8.072}
    for name, (base, spread) in spreads.items():
        noise = np.random.default_rng([zlib.crc32(name.encode()), seed]).standard_normal(out[name].shape)
        drawn = base * np.exp(spread * noise) if base else spread * noise
        out[name] = __import__('jax').numpy.asarray(drawn.astype(out[name].dtype))
    for name, factor in factors.items():
        out[name] = (out[name] * factor).astype(out[name].dtype)
    return out
```

```python
from collections import namedtuple
from contextlib import ExitStack

import numpy as np

import concourse.bass as bass
from concourse import mybir

F32 = mybir.dt.float32
F32R = mybir.dt.float32r
ALU = mybir.AluOpType
ACT = mybir.ActivationFunctionType

P = 128
D = 2048
S = 256
DEPTH = 2
HEADS = 16
HALF_DIM = 64
D_FF = 5632
EPS = 1e-5
LAMBDA_INIT = 0.2
N_BUCKETS, MAX_DISTANCE = 32, 128
MASKED = -1e30
LN_EXP = "natural_log_exp_and_others"

XT = D // P
CHUNKS = (16, 16, 12)
assert sum(CHUNKS) * P == D_FF
FULL, SHORT = 16, 12

HEAD_UNITS = 3 * HEADS
O_BASE = HEAD_UNITS
FFN_BASE = O_BASE + XT
GU_BASE, DOWN_BASE = [], []
_u = FFN_BASE
for _c in CHUNKS:
    GU_BASE.append(_u)
    DOWN_BASE.append(_u + 2 * _c)
    _u += 2 * _c + XT
UNITS_PER_LAYER = _u
FULL_PER_LAYER = UNITS_PER_LAYER - XT
SLOTS = 4
TOK = S // P

Unit = namedtuple("Unit", "n slot lap")


def unit(base, per_group, g, off):
    return Unit(base + per_group * g + off, off % SLOTS,
                base // SLOTS + per_group // SLOTS * g + off // SLOTS)


def wait(eng, sem, value):
    if not (isinstance(value, int) and value <= 0):
        eng.wait_ge(sem, value)


def stand_alone(eng):
    eng.nop(nofuse=True)


def for_groups(eng, n, body, peel_first=False, peel_last=False):
    lo, hi = (1 if peel_first else 0), (n - 1 if peel_last else n)
    if peel_first:
        body(0)
    if hi > lo:
        with eng.Fori(lo, hi) as g:
            body(g)
    if peel_last:
        body(n - 1)


def last_two(g, n_groups, j):
    return isinstance(g, int) and g == n_groups - 1 and j >= SLOTS - 2


X_START = XT
X_HEADS = [0, 0]
X_O = [0, 0]
X_ACT = [[0] * 3, [0] * 3]
_x = X_START
for _l in range(DEPTH):
    _x += HEADS
    X_HEADS[_l] = _x
    _x += XT
    X_O[_l] = _x
    for _i, _c in enumerate(CHUNKS):
        _x += _c
        X_ACT[_l][_i] = _x
    if _l == 0:
        _x += 2 * XT
X_DOWN0 = X_ACT[0][2] + 2 * XT
G_ATTN, G_FFN, G_KV, G_FINAL, G_SUBLN = (0, 16), (32, 48), 64, 80, 96
N_GAINS = 97


def trunk(nc, w_full, w_short, x, gains, lambdas, rel_bias, bucket_rows, bias_rows, out):
    ctx = ExitStack()
    with ctx:
        def sb(name, shape, dt=F32):
            return ctx.enter_context(nc.sbuf_tensor(name, shape, dt))

        def sem(name):
            return ctx.enter_context(nc.semaphore(name))

        raw = sb("raw", [P, SLOTS, FULL * P])
        w_hi = sb("w_hi", [P, 4, FULL * P // 2], F32R)
        w_lo = sb("w_lo", [P, 4, FULL * P // 2], F32R)
        xa = sb("xa", [P, XT, 2 * S], F32R)
        xb = sb("xb", [P, XT, 2 * S], F32R)
        xc = sb("xc", [P, XT, 2 * S], F32R)
        h = sb("h", [P, XT, S])
        tmp = sb("tmp", [P, 2, S])
        total = sb("total", [P, 2, S])
        rs = sb("rs", [P, S])
        rs_q = sb("rs_q", [P, S])
        ssq = sb("ssq", [P, S])
        sq = sb("sq", [P, S])
        ident = sb("ident", [P, P])
        ones = sb("ones", [P, P])
        neg_tri = sb("neg_tri", [P, P])
        neg_ones = sb("neg_ones", [P, P])
        gain = sb("gain", [P, N_GAINS])
        gain_sub = sb("gain_sub", [P, 1])
        eps = sb("eps", [P, 1])
        lam_in = sb("lam_in", [P, 4, HALF_DIM])
        lam_s = sb("lam_s", [P, 8])
        bias = sb("bias", [P, 2, S])
        q_t = sb("q_t", [P, S])
        k_t = sb("k_t", [P, S])
        v_t = sb("v_t", [P, S])
        v_tok = sb("v_tok", [P, S])
        sc = sb("sc", [P, 2, 3 * P])
        a_t = sb("a_t", [P, 3 * P])
        small = sb("small", [P, 20])
        o_raw = sb("o_raw", [P, S])
        o_sq = sb("o_sq", [P, S])
        o_rs = sb("o_rs", [P, S])
        gate = q_t
        gate_silu = k_t
        gate_w = o_raw
        hidden = o_sq
        rel_ext = sc[0:N_BUCKETS + 1, 0, 0:HEADS]
        onehot = sc[0:N_BUCKETS + 1, 1, 0:3 * P]
        rows_sb = a_t[0:HEADS, :]

        bank = [ctx.enter_context(nc.psum_tensor(f"bank{i}", [P, 512], F32)) for i in range(SLOTS)]
        ps_s = [ctx.enter_context(nc.psum_tensor(f"ps_s{i}", [P, 512], F32)) for i in range(2)]
        ps_x = ctx.enter_context(nc.psum_tensor("ps_x", [P, 512], F32))
        ps_y = ctx.enter_context(nc.psum_tensor("ps_y", [P, 512], F32))
        all_banks = [bank[0], ps_y, ps_x] + ps_s + bank[1:]

        landed = [sem(f"landed{i}") for i in range(SLOTS)]
        x_landed = [sem(f"x_landed{i}") for i in range(4)]
        consts_landed = sem("consts_landed")
        rows_landed = sem("rows_landed")
        rows_stored = sem("rows_stored")
        bias_landed = [sem(f"bias_landed{i}") for i in range(2)]
        out_stored = sem("out_stored")
        consts_made = sem("consts_made")
        rel_made = sem("rel_made")
        rows_full = sem("rows_full")
        rows_copied = sem("rows_copied")
        turned_in = sem("turned_in")
        h_made = sem("h_made")
        hi_ready = sem("hi_ready")
        lo_ready = sem("lo_ready")
        used = sem("used")
        tmp_ready = sem("tmp_ready")
        summed = sem("summed")
        took = sem("took")
        x_hi = sem("x_hi")
        x_lo = sem("x_lo")
        sq_ready = sem("sq_ready")
        ssq_added = sem("ssq_added")
        ssq_zeroed = sem("ssq_zeroed")
        norm_full = sem("norm_full")
        norm_ln = sem("norm_ln")
        rs_ready = sem("rs_ready")
        scores_full = sem("scores_full")
        max_ready = sem("max_ready")
        exp_ready = sem("exp_ready")
        dve_chain = sem("dve_chain")
        bias_chain = sem("bias_chain")
        a_ready = sem("a_ready")
        a_turned = sem("a_turned")
        a_copied = sem("a_copied")
        v_turned = sem("v_turned")
        v_copied = sem("v_copied")
        o_full = sem("o_full")
        o_copied = sem("o_copied")
        o_squared = sem("o_squared")
        o_ss = sem("o_ss")
        o_ln = sem("o_ln")
        o_rs_ready = sem("o_rs_ready")
        o_normed = sem("o_normed")
        lam_sums = sem("lam_sums")
        lam_exps = sem("lam_exps")
        lam_made = sem("lam_made")
        sub_made = sem("sub_made")
        sp_parts = sem("sp_parts")
        act_chain = sem("act_chain")
        sp_ready = sem("sp_ready")
        sp_masked = sem("sp_masked")
        cum_full = sem("cum_full")
        stick_exp = sem("stick_exp")
        stick_masked = sem("stick_masked")
        silu_ready = sem("silu_ready")
        pool_chain = sem("pool_chain")
        w_ready = sem("w_ready")
        y_made = sem("y_made")
        y_turned = sem("y_turned")
        y_copied = sem("y_copied")

        def half(u, s):
            return (2 * u.slot + s) % 4

        def x_tile(buf, t):
            if isinstance(t, int):
                return buf[:, t, 0:S], buf[:, t, S:2 * S]
            return (buf[:, bass.ds(t, 1), 0:S].rearrange("p a s -> p (a s)"),
                    buf[:, bass.ds(t, 1), S:2 * S].rearrange("p a s -> p (a s)"))

        def h_tile(t):
            return h[:, t, :] if isinstance(t, int) else h[:, bass.ds(t, 1), :].rearrange("p a s -> p (a s)")

        def g_col(base, t):
            return gain[:, base + t:base + t + 1] if isinstance(t, int) else gain[:, bass.ds(base + t, 1)]

        def feeds(layer, section):
            if section == "o":
                return [(xa, G_FFN[layer])]
            return [(xa, G_ATTN[1]), (xb, G_KV)] if layer == 0 else []

        block = ctx.enter_context(nc.Block())

        @block.sync
        def _(sp):
            x_fourth = D // 4
            for c in range(4):
                cols = slice(c * x_fourth, (c + 1) * x_fourth)
                sp.dma_start(raw[:, 2:4, cols], x[:, cols].rearrange("(t p) d -> p t d", p=P))\
                  .then_inc(x_landed[c], 16)
                if c == 0:
                    sp.dma_start(gain[:, :], gains).then_inc(consts_landed, 16)
                    sp.dma_start(lam_in[:, :, :], lambdas.partition_broadcast(P)).then_inc(consts_landed, 16)
                if c == 2:
                    sp.dma_start(raw[:, 0, :], w_full[0]).then_inc(landed[0], 16)
            sp.dma_start(sc[0:N_BUCKETS, 0, 0:HEADS], rel_bias).then_inc(rows_landed, 16)
            sp.dma_start(onehot, bucket_rows).then_inc(rows_landed, 16)

            def load(u, row, src):
                wait(sp, lo_ready, 2 * (u.n - SLOTS) + 2)
                width = FULL * P if src is w_full else SHORT * P
                sp.dma_start(raw[:, u.slot, 0:width], src[row]).then_inc(landed[u.slot], 16)

            def load_bias(head, b):
                wait(sp, max_ready, 2 * (head - 1))
                rows = bass.AP(tensor=bias_rows.tensor, offset=head * 3 * P, ap=[[1, P], [1, S]])
                sp.dma_start(bias[:, b, :], rows).then_inc(bias_landed[b], 16)

            def head_group(g):
                for j in range(4):
                    for r in range(3):
                        u = unit(0, 12, g, 3 * j + r)
                        if isinstance(g, int) and u.n in (2, 3):
                            wait(sp, turned_in, XT // 2)
                        if not (isinstance(g, int) and u.n == 0):
                            load(u, u.n, w_full)
                    if isinstance(g, int) and j == 0:
                        sp.wait_ge(rows_copied, 1)
                        sp.dma_start(bias_rows, rows_sb).then_inc(rows_stored, 16)
                        sp.wait_ge(rows_stored, 16)
                    load_bias(4 * g + j, j % 2)

            for_groups(sp, HEADS // 4, head_group, peel_first=True)
            for layer in range(DEPTH):
                base = layer * UNITS_PER_LAYER
                first = HEAD_UNITS if layer == 0 else 0

                def group(g, base=base + first, row=layer * FULL_PER_LAYER + first):
                    for j in range(SLOTS):
                        load(unit(base, SLOTS, g, j), row + SLOTS * g + j, w_full)

                def short_group(g, base=base + FULL_PER_LAYER, row=layer * XT):
                    for j in range(SLOTS):
                        load(unit(base, SLOTS, g, j), row + SLOTS * g + j, w_short)

                for_groups(sp, (FULL_PER_LAYER - first) // SLOTS, group)
                for_groups(sp, XT // SLOTS, short_group)
            for b in range(4):
                for t in range(TOK):
                    sp.wait_ge(y_copied, TOK * b + t + 1)
                    sp.dma_start(out[t * P:(t + 1) * P, b * 512:(b + 1) * 512],
                                 raw[:, t, b * 512:(b + 1) * 512]).then_inc(out_stored, 16)
            sp.wait_ge(out_stored, 16 * 4 * TOK)

        @block.tensor
        def _(pe):
            mm = nc.tensor.matmul

            def tile_products(b, u, i, kt, x_buf, n_half, first, last):
                s, o = i // n_half, i % n_half * P
                k = half(u, s)
                mm(bank[b][:, :], w_hi[:, k, o:o + P], x_buf[:, kt, :], start=first, stop=False)
                return mm(bank[b][:, 0:S], w_lo[:, k, o:o + P], x_buf[:, kt, 0:S], start=False, stop=last)

            def products(u, x_buf, n_tiles, x_count, per_tile=0):
                pe_half = n_tiles // 2
                wait(pe, summed, u.n - SLOTS + 1)
                for kt in range(n_tiles):
                    if kt % pe_half == 0:
                        wait(pe, lo_ready, 2 * u.n + kt // pe_half + 1)
                    if per_tile:
                        pe.wait_ge(x_lo, x_count - per_tile * (n_tiles - 1 - kt))
                    elif kt == 0:
                        pe.wait_ge(x_lo, x_count - 1)
                    elif kt == n_tiles - 1:
                        pe.wait_ge(x_lo, x_count)
                    last = tile_products(u.slot, u, kt, kt, x_buf, pe_half, kt == 0, kt == n_tiles - 1)
                    if kt % pe_half == pe_half - 1:
                        last.then_inc(used, 1)

            def norm_sum(n):
                pe.wait_ge(ssq_added, XT * (n + 1))
                wait(pe, o_ln, HEADS if n >= 1 else 0)
                wait(pe, rs_ready, n)
                mm(ps_x[:, 0:S], ones[:, :], ssq[:, :], start=True, stop=True).then_inc(norm_full, 1)

            def turn_v(i, layer):
                n = HEADS * layer + i
                pe.wait_ge(took, UNITS_PER_LAYER * layer + 3 * i + 3)
                if layer == 0:
                    wait(pe, o_copied, i)
                else:
                    wait(pe, x_lo, X_DOWN0 + i)
                for t in range(TOK):
                    last = nc.tensor.transpose(ps_y[:, t * P:(t + 1) * P], v_t[:, t * P:(t + 1) * P], ident[:, :])
                last.then_inc(v_turned, 1)

            def weigh_v(i, layer):
                n = HEADS * layer + i
                pe.wait_ge(v_copied, n + 1)
                if layer == 0:
                    pe.wait_ge(a_copied, i + 1)
                else:
                    pe.wait_ge(stick_masked, i + 1)
                mm(ps_y[:, 0:S], v_tok[:, 0:P], a_t[:, 0:S], start=True, stop=False)
                mm(ps_y[:, P:S], v_tok[:, P:2 * P], a_t[:, S:S + P], start=False, stop=True).then_inc(o_full, 1)

            def attention0(r, i):
                new = not isinstance(i, int) or i < HEADS
                prev = not isinstance(i, int) or 1 <= i <= HEADS
                prev2 = not isinstance(i, int) or i >= 2
                if r == 0:
                    if prev:
                        turn_v(i - 1, 0)
                    if prev2:
                        pe.wait_ge(o_squared, i - 1)
                        wait(pe, a_copied, i - 1)
                        mm(ps_x[:, 0:S], ones[:, :], o_sq[:, :], start=True, stop=True).then_inc(o_ss, 1)
                elif r == 1 and prev:
                    pe.wait_ge(a_ready, i)
                    wait(pe, o_ln, i - 1)
                    wait(pe, norm_ln, 1)
                    for b in range(3):
                        last = nc.tensor.transpose(ps_x[:, b * P:(b + 1) * P], sc[:, 0, b * P:(b + 1) * P], ident[:, :])
                    last.then_inc(a_turned, 1)
                elif r == 2:
                    if prev:
                        weigh_v(i - 1, 0)
                    if new:
                        pe.wait_ge(took, 3 * i + 2)
                        wait(pe, max_ready, 2 * i)
                        for m in range(2):
                            rows = slice(m * HALF_DIM, (m + 1) * HALF_DIM)
                            mm(ps_s[m][:, 0:P], q_t[rows, 0:P], k_t[rows, 0:P], start=True, stop=True)
                            last = mm(ps_s[m][:, P:3 * P], q_t[rows, P:S], k_t[rows, :], start=True, stop=True,
                                      skip_group_check=True)
                            last.then_inc(scores_full, 1)

            def attention1(r, i):
                new = not isinstance(i, int) or i < HEADS
                prev = not isinstance(i, int) or 1 <= i <= HEADS
                if r == 0 and prev:
                    turn_v(i - 1, 1)
                    pe.wait_ge(sp_masked, i)
                    mm(ps_s[0][:, 0:S], neg_tri[:, :], sc[:, 0, 0:S], start=False, stop=False, skip_group_check=True)
                    mm(ps_s[0][:, P:S], neg_ones[:, :], sc[:, 0, S:3 * P], start=False, stop=False,
                       skip_group_check=True)
                    mm(ps_s[0][:, S:3 * P], neg_tri[:, :], sc[:, 0, S:3 * P], start=False, stop=True,
                       skip_group_check=True).then_inc(cum_full, 1)
                elif r == 2:
                    if prev:
                        weigh_v(i - 1, 1)
                    if new:
                        pe.wait_ge(took, UNITS_PER_LAYER + 3 * i + 2)
                        wait(pe, stick_exp, i)
                        mm(ps_s[0][:, 0:S], k_t[:, 0:P], q_t[:, :], start=True, stop=True, skip_group_check=True)
                        mm(ps_s[0][:, S:3 * P], k_t[:, P:S], q_t[:, P:S], start=False, stop=True,
                           skip_group_check=True).then_inc(scores_full, 1)

            pe.wait_ge(consts_made, 1)
            for t in range(XT):
                if t % 4 == 0:
                    pe.wait_ge(x_landed[t // 4], 16)
                for k in range(TOK):
                    last = nc.tensor.transpose(all_banks[t // 2][:, (t % 2 * TOK + k) * P:(t % 2 * TOK + k + 1) * P],
                                               raw[:, 2 + k, t * P:(t + 1) * P], ident[:, :])
                if t % 2 == 1:
                    last.then_inc(turned_in, 1)
            pe.wait_ge(rel_made, 1)
            pe.wait_ge(rows_landed, 32)
            pe.wait_ge(h_made, 2)
            mm(ps_y[0:HEADS, 0:3 * P], rel_ext, onehot, start=True, stop=True).then_inc(rows_full, 1)

            for layer in range(DEPTH):
                base = layer * UNITS_PER_LAYER
                attention = attention0 if layer == 0 else attention1

                def head_group(g):
                    for j in range(4):
                        i = 4 * g + j
                        for r in range(3):
                            kv = layer == 1 and r > 0
                            first = isinstance(g, int) and j == 0 and r == 0
                            products(unit(base, 12, g, 3 * j + r), xb if kv else xa, FULL,
                                     X_START if layer == 0 else X_DOWN0, (layer + 1) * first)
                            if first:
                                norm_sum(2 * layer)
                            attention(r, i)

                for_groups(pe, HEADS // 4, head_group, peel_first=True)

                heads_out = xb if layer == 0 else xc
                for a in range(4):
                    u = unit(base + O_BASE, SLOTS, 0, a)
                    for kk in range(4):
                        kt = 4 * a + kk
                        if kt == XT - 1:
                            if layer == 0:
                                attention(0, HEADS + 1)
                        wait(pe, x_lo, X_HEADS[layer] - XT + kt + 1)
                        if kk % 2 == 0:
                            pe.wait_ge(lo_ready, 2 * u.n + kk // 2 + 1)
                        for n in range(4):
                            if kt == 0:
                                pe.wait_ge(summed, u.n + n - SLOTS + 1)
                            last = tile_products(n, u, 4 * kk + n, kt, heads_out, 8, kt == 0, kt == XT - 1)
                        if kk % 2 == 1:
                            last.then_inc(used, 1)
                    if a < 3:
                        attention(a, HEADS)

                def o_group(g):
                    for j in range(SLOTS):
                        products(unit(base + O_BASE, SLOTS, g, j), heads_out, FULL, X_HEADS[layer])

                with pe.Fori(1, XT // SLOTS) as g:
                    o_group(g)

                for c, tiles in enumerate(CHUNKS):
                    def gu_group(g):
                        for j in range(SLOTS):
                            first = c == 0 and isinstance(g, int) and j == 0
                            products(unit(base + GU_BASE[c], SLOTS, g, j), xa, FULL, X_O[layer], int(first))
                            if first:
                                norm_sum(2 * layer + 1)

                    def down_group(g):
                        for j in range(SLOTS):
                            products(unit(base + DOWN_BASE[c], SLOTS, g, j), xc, tiles, X_ACT[layer][c])

                    for_groups(pe, 2 * tiles // SLOTS, gu_group, peel_first=c == 0)
                    for_groups(pe, XT // SLOTS, down_group)

            norm_sum(4)
            for t in range(XT):
                b = t // 4 % 4
                pe.wait_ge(y_made, t + 1)
                for k in range(TOK):
                    dst = (bank + ps_s + [ps_x, ps_y])[4 * k + b]
                    if t % 4 == 0 and k == 1 and b == 2:
                        pe.wait_ge(rs_ready, 5)
                    last = nc.tensor.transpose(dst[:, t % 4 * P:(t % 4 + 1) * P], h[:, t, k * P:(k + 1) * P],
                                               ident[:, :])
                if t % 4 == 3:
                    last.then_inc(y_turned, 1)

        @block.scalar
        def _(act):
            f = nc.scalar.activation

            def split(u, tiles):
                w = tiles // 2 * P
                for s in range(2):
                    if s == 0:
                        act.wait_ge(landed[u.slot], 16 * u.lap + 16)
                    wait(act, used, 2 * u.n + s - 3)
                    f(w_hi[:, half(u, s), 0:w], raw[:, u.slot, s * w:(s + 1) * w], ACT.Copy).then_inc(hi_ready, 1)

            def read_out(u, full=None):
                act.wait_ge(used, 2 * u.n + 2 if full is None else full)
                wait(act, summed, u.n - 1)
                f(tmp[:, u.slot % 2, :], bank[u.slot][:, S:2 * S], ACT.Copy).then_inc(tmp_ready, 1)

            def feed(n, dst, count):
                for d, (buf, g) in enumerate(dst):
                    stand_alone(act)
                    f(x_tile(buf, n)[0], h_tile(n), ACT.Copy, scale=g_col(g, n)).then_inc(x_hi, 1)

            def square(n, done):
                wait(act, ssq_added, done)
                stand_alone(act)
                f(sq[:, :], h_tile(n), ACT.Square).then_inc(sq_ready, 1)

            def norm_scale(n, q_scale):
                act.wait_ge(norm_full, n + 1)
                f(ssq_ln, ps_x[:, 0:S], ACT.Ln, bias=eps[:, 0:1], scale=1.0 / D).then_inc(norm_ln, 1)
                act.wait_ge(norm_ln, n + 1)
                f(rs[:, :], ssq_ln, ACT.Exp, scale=-0.5).then_inc(act_chain, 1)
                act.wait_ge(act_chain, chain_next())
                f(rs_q[:, :], rs[:, :], ACT.Copy, scale=q_scale).then_inc(rs_ready, 1)

            ssq_ln = rs_q[:, :]
            chain = [0]

            def chain_next():
                chain[0] += 1
                return chain[0]

            def attention0(r, i):
                new = not isinstance(i, int) or i < HEADS
                prev = not isinstance(i, int) or 1 <= i <= HEADS
                prev2 = not isinstance(i, int) or i >= 2
                if r == 0:
                    if prev:
                        act.wait_ge(v_turned, i)
                        wait(act, o_full, i - 1)
                        f(v_tok[:, :], ps_y[:, 0:S], ACT.Copy).then_inc(v_copied, 1)
                    if prev2:
                        act.wait_ge(o_ss, i - 1)
                        wait(act, o_normed, i - 2)
                        f(o_sq[:, :], ps_x[:, 0:S], ACT.Ln, bias=eps[:, 0:1], scale=1.0 / P).then_inc(o_ln, 1)
                        act.wait_ge(o_ln, i - 1)
                        f(o_rs[:, :], o_sq[:, :], ACT.Exp, scale=-0.5).then_inc(o_rs_ready, 1)
                elif r == 1 and prev2:
                    act.wait_ge(o_normed, i - 1)
                    stand_alone(act)
                    f(x_tile(xb, i - 2)[0], o_rs[:, :], ACT.Copy, scale=gain_sub[:, 0:1]).then_inc(x_hi, 1)
                elif r == 2:
                    if prev:
                        act.wait_ge(o_copied, i)
                        wait(act, o_rs_ready, i - 1)
                        f(o_sq[:, :], o_raw[:, :], ACT.Square).then_inc(o_squared, 1)
                    if new:
                        for m in range(2):
                            act.wait_ge(max_ready, 2 * i + m + 1)
                            for q, cols in enumerate((slice(0, P), slice(P, 3 * P))):
                                c = 2 * m + q
                                last = f(sc[:, m, cols], sc[:, m, cols], ACT.Exp, bias=small[:, c:c + 1],
                                         accum_out=small[:, 4 + c:5 + c])
                            last.then_inc(exp_ready, 1)

            def attention1(r, i):
                new = not isinstance(i, int) or i < HEADS
                prev = not isinstance(i, int) or 1 <= i <= HEADS
                if r == 0 and prev:
                    act.wait_ge(v_turned, HEADS + i)
                    wait(act, o_full, HEADS + i - 1)
                    f(v_tok[:, :], ps_y[:, 0:S], ACT.Copy).then_inc(v_copied, 1)
                    act.wait_ge(cum_full, i)
                    f(a_t[:, :], ps_s[0][:, 0:3 * P], ACT.Exp).then_inc(stick_exp, 1)
                elif r == 2:
                    if prev:
                        act.wait_ge(o_full, HEADS + i)
                        stand_alone(act)
                        f(x_tile(xc, i - 1)[0], ps_y[:, 0:S], ACT.Copy).then_inc(x_hi, 1)
                    if new:
                        act.wait_ge(scores_full, 2 * HEADS + i + 1)
                        wait(act, cum_full, i)
                        f(sc[:, 1, :], ps_s[0][:, 0:3 * P], ACT.Abs).then_inc(sp_parts, 1)
                        act.wait_ge(sp_parts, 3 * i + 1)
                        f(sc[:, 1, :], sc[:, 1, :], ACT.Exp, scale=-1.0).then_inc(sp_parts, 1)
                        act.wait_ge(sp_parts, 3 * i + 2)
                        f(sc[:, 1, :], sc[:, 1, :], ACT.Ln, bias=1.0).then_inc(sp_parts, 1)

            nc.scalar.preload_act_table_set(LN_EXP)
            act.wait_ge(consts_landed, 32)
            act.wait_ge(lam_sums, 2)
            f(lam_s[:, 2:4], lam_s[:, 0:2], ACT.Exp).then_inc(lam_exps, 1)
            f(gain_sub[:, 0:1], gain[:, G_SUBLN:G_SUBLN + 1], ACT.Copy, scale=1.0 - LAMBDA_INIT).then_inc(sub_made, 1)
            act.wait_ge(ssq_zeroed, 1)
            for t in range(XT):
                act.wait_ge(h_made, t // 2 + 1)
                feed(t, [(xa, G_ATTN[0])], t)
                square(t, t)
                if t == 7:
                    split(unit(0, SLOTS, 0, 0), FULL)
            split(unit(0, SLOTS, 0, 1), FULL)

            for layer in range(DEPTH):
                base = layer * UNITS_PER_LAYER
                attention = attention0 if layer == 0 else attention1
                if layer > 0:
                    nc.scalar.preload_act_table_set(LN_EXP)

                def head_group(g):
                    for j in range(4):
                        for r in range(3):
                            off = 3 * j + r
                            read_out(unit(base, 12, g, off))
                            if isinstance(g, int) and off == 0:
                                norm_scale(2 * layer, (HALF_DIM if layer == 0 else P) ** -0.5)
                            split(unit(base, 12, g, off + 2), FULL)
                            attention(r, 4 * g + j)

                for_groups(act, HEADS // 4, head_group, peel_first=True)

                def residual_unit(u, n, next_tiles, dst, norm, full=None, other=None):
                    read_out(u, full)
                    if other is not None and n == 0:
                        split(other, FULL)
                    if next_tiles:
                        split(Unit(u.n + 2, (u.slot + 2) % SLOTS, u.lap + (u.slot + 2) // SLOTS), next_tiles)
                    if norm is not None:
                        act.wait_ge(took, u.n + 1)
                        feed(n, dst, 0)
                        square(n, XT * norm + n)

                for a in range(3):
                    split(unit(base + O_BASE, SLOTS, 0, a + 2), FULL)
                    attention(a, HEADS)
                if layer == 0:
                    attention(0, HEADS + 1)
                    attention(1, HEADS + 1)
                for n in range(4):
                    residual_unit(unit(base + O_BASE, SLOTS, 0, n), n, 0, feeds(layer, "o"), 2 * layer + 1,
                                  2 * (base + O_BASE) + 2 * SLOTS, unit(base + O_BASE, SLOTS, 1, 1))
                with act.Fori(1, XT // SLOTS) as g:
                    for j in range(SLOTS):
                        residual_unit(unit(base + O_BASE, SLOTS, g, j), SLOTS * g + j, FULL, feeds(layer, "o"),
                                      2 * layer + 1)

                for c, tiles in enumerate(CHUNKS):
                    last_chunk = c == len(CHUNKS) - 1
                    n_groups = 2 * tiles // SLOTS
                    pairs = base // UNITS_PER_LAYER * sum(CHUNKS) + sum(CHUNKS[:c])

                    def gu_group(g):
                        for j in range(SLOTS):
                            u = unit(base + GU_BASE[c], SLOTS, g, j)
                            read_out(u)
                            if c == 0 and isinstance(g, int) and g == 0 and j == 0:
                                norm_scale(2 * layer + 1, 1.0)
                            split(unit(base + GU_BASE[c], SLOTS, g, j + 2),
                                  SHORT if last_chunk and last_two(g, n_groups, j) else FULL)
                            act.wait_ge(took, u.n + 1)
                            pair = 2 * g + j // 2
                            if j % 2 == 0:
                                f(gate_silu[:, :], gate[:, :], ACT.Silu).then_inc(silu_ready, 1)
                            else:
                                stand_alone(act)
                                f(x_tile(xc, pair)[0], hidden[:, :], ACT.Copy).then_inc(x_hi, 1)

                    for_groups(act, n_groups, gu_group, peel_first=c == 0, peel_last=last_chunk)
                    norm = 2 * layer + 2 if last_chunk else None
                    n_down = XT // SLOTS

                    def down_group(g):
                        for j in range(SLOTS):
                            if not last_chunk:
                                nxt = FULL
                            elif last_two(g, n_down, j):
                                nxt = 0 if layer == DEPTH - 1 else FULL
                            else:
                                nxt = SHORT
                            residual_unit(unit(base + DOWN_BASE[c], SLOTS, g, j), SLOTS * g + j, nxt,
                                          feeds(layer, "down"), norm)

                    for_groups(act, n_down, down_group, peel_last=last_chunk)

            nc.scalar.preload_act_table_set(LN_EXP)
            norm_scale(4, 1.0)
            spare = (bank + ps_s + [ps_x, ps_y])
            for b in range(4):
                act.wait_ge(y_turned, b + 1)
                for k in range(TOK):
                    f(raw[:, k, b * 512:(b + 1) * 512], spare[4 * k + b][:, :], ACT.Copy).then_inc(y_copied, 1)

        @block.vector
        def _(dve):
            v = nc.vector

            def split(u, tiles):
                w = tiles // 2 * P
                for s in range(2):
                    dve.wait_ge(hi_ready, 2 * u.n + s + 1)
                    k = half(u, s)
                    v.tensor_tensor(w_lo[:, k, 0:w], raw[:, u.slot, s * w:(s + 1) * w],
                                    w_hi[:, k, 0:w].bitcast(F32), ALU.subtract).then_inc(lo_ready, 1)

            def read_out(u):
                dve.wait_ge(tmp_ready, u.n + 1)
                wait(dve, took, u.n - 1)
                v.tensor_tensor(total[:, u.slot % 2, :], bank[u.slot][:, 0:S], tmp[:, u.slot % 2, :],
                                ALU.add).then_inc(summed, 1)

            def feed(n, dst, count):
                for d, (buf, g) in enumerate(dst):
                    hi, lo = x_tile(buf, n)
                    dve.wait_ge(x_hi, count + d + 1)
                    v.scalar_tensor_tensor(lo, h_tile(n), g_col(g, n), hi.bitcast(F32),
                                           ALU.mult, ALU.subtract).then_inc(x_lo, 1)

            def attention0(r, i, b=0, lap=0):
                new = not isinstance(i, int) or i < HEADS
                prev = not isinstance(i, int) or 1 <= i <= HEADS
                prev2 = not isinstance(i, int) or i >= 2
                if r == 0 and prev:
                    dve.wait_ge(exp_ready, 2 * i)
                    v.reciprocal(small[:, 8:12], small[:, 4:8]).then_inc(dve_chain, 1)
                    dve.wait_ge(dve_chain, 3 * (i - 1) + 1)
                    v.tensor_scalar(small[:, 12:14], small[:, 10:12], lam_s[:, 5:6], None, ALU.mult)\
                     .then_inc(dve_chain, 1)
                    dve.wait_ge(dve_chain, 3 * (i - 1) + 2)
                    for q, cols in enumerate((slice(0, P), slice(P, 3 * P))):
                        last = v.tensor_scalar(sc[:, 1, cols], sc[:, 1, cols], small[:, 12 + q:13 + q], None, ALU.mult)
                    last.then_inc(dve_chain, 1)
                    dve.wait_ge(dve_chain, 3 * (i - 1) + 3)
                    for q, cols in enumerate((slice(0, P), slice(P, 3 * P))):
                        last = v.scalar_tensor_tensor(sc[:, 0, cols], sc[:, 0, cols], small[:, 8 + q:9 + q],
                                                      sc[:, 1, cols], ALU.mult, ALU.add)
                    last.then_inc(a_ready, 1)
                elif r == 1:
                    if prev:
                        dve.wait_ge(a_turned, i)
                        wait(dve, o_full, i - 1)
                        v.tensor_copy(a_t[:, :], ps_x[:, 0:3 * P]).then_inc(a_copied, 1)
                    if prev2:
                        hi, lo = x_tile(xb, i - 2)
                        dve.wait_ge(x_hi, X_START + i - 1)
                        v.scalar_tensor_tensor(lo, o_rs[:, :], gain_sub[:, 0:1], hi.bitcast(F32),
                                               ALU.mult, ALU.subtract).then_inc(x_lo, 1)
                elif r == 2:
                    if prev:
                        dve.wait_ge(o_full, i)
                        wait(dve, o_normed, i - 1)
                        v.tensor_copy(o_raw[:, :], ps_y[:, 0:S]).then_inc(o_copied, 1)
                    if new:
                        biased_scores(i, b, lap)

            def biased_scores(i, b, lap):
                dve.wait_ge(bias_landed[b], 16 * lap + 16)
                wait(dve, a_turned, i)
                rev = bias[:, b, :]
                rev = bass.AP(tensor=rev.tensor, offset=rev.offset + S - 1, ap=[rev.ap[0], [-1, S]])
                for m in range(2):
                    dve.wait_ge(scores_full, 2 * i + m + 1)
                    stand_alone(dve)
                    v.tensor_tensor_reduce(sc[:, m, 0:P], ps_s[m][:, 0:P], rev[:, P:S], 1.0, MASKED,
                                           ALU.add, ALU.max, small[:, 14 + 2 * m:15 + 2 * m])
                    last = v.tensor_tensor_reduce(sc[:, m, P:3 * P], ps_s[m][:, P:3 * P], rev[:, :], 1.0, MASKED,
                                                  ALU.add, ALU.max, small[:, 15 + 2 * m:16 + 2 * m])
                    last.then_inc(bias_chain, 1)
                    dve.wait_ge(bias_chain, 2 * i + m + 1)
                    v.tensor_scalar(small[:, 2 * m:2 * m + 2], small[:, 14 + 2 * m:16 + 2 * m], -1.0, None, ALU.mult)\
                     .then_inc(max_ready, 1)

            def attention1(r, i, b=0, lap=0):
                new = not isinstance(i, int) or i < HEADS
                prev = not isinstance(i, int) or 1 <= i <= HEADS
                if r == 2:
                    if prev:
                        hi, lo = x_tile(xc, i - 1)
                        dve.wait_ge(x_hi, X_DOWN0 + i)
                        v.tensor_tensor(lo, ps_y[:, 0:S], hi.bitcast(F32), ALU.subtract).then_inc(x_lo, 1)
                    if new:
                        dve.wait_ge(sp_parts, 3 * i + 3)
                        v.scalar_tensor_tensor(sc[:, 0, :], ps_s[0][:, 0:3 * P], 0.0, sc[:, 1, :],
                                               ALU.max, ALU.add).then_inc(sp_ready, 1)

            v.memset(sc[N_BUCKETS:N_BUCKETS + 1, 0, 0:HEADS], MASKED).then_inc(rel_made, 1)
            dve.wait_ge(consts_landed, 32)
            for m in range(2):
                v.tensor_tensor_reduce(lam_in[:, 2 * m, :], lam_in[:, 2 * m, :], lam_in[:, 2 * m + 1, :], 1.0, 0.0,
                                       ALU.mult, ALU.add, lam_s[:, m:m + 1]).then_inc(lam_sums, 1)
            for t in range(XT // 2):
                dve.wait_ge(turned_in, t + 1)
                v.tensor_copy(h[:, 2 * t:2 * t + 2, :].rearrange("p a s -> p (a s)"), all_banks[t][:, :])\
                 .then_inc(h_made, 1)
                for n in (2 * t, 2 * t + 1):
                    dve.wait_ge(h_made, t + 1)
                    feed(n, [(xa, G_ATTN[0])], n)
                if t == 3:
                    split(unit(0, SLOTS, 0, 0), FULL)
            split(unit(0, SLOTS, 0, 1), FULL)
            dve.wait_ge(rows_full, 1)
            v.tensor_copy(rows_sb, ps_y[0:HEADS, 0:3 * P]).then_inc(rows_copied, 1)
            dve.wait_ge(lam_exps, 1)
            v.tensor_tensor(lam_s[:, 4:5], lam_s[:, 3:4], lam_s[:, 2:3], ALU.subtract).then_inc(lam_made, 1)
            dve.wait_ge(lam_made, 1)
            v.tensor_scalar(lam_s[:, 5:6], lam_s[:, 4:5], -LAMBDA_INIT, None, ALU.add).then_inc(lam_made, 1)
            dve.wait_ge(lam_made, 2)
            dve.wait_ge(sub_made, 1)

            for layer in range(DEPTH):
                base = layer * UNITS_PER_LAYER
                attention = attention0 if layer == 0 else attention1

                def head_group(g):
                    for j in range(4):
                        for r in range(3):
                            read_out(unit(base, 12, g, 3 * j + r))
                            split(unit(base, 12, g, 3 * j + r + 2), FULL)
                            attention(r, 4 * g + j, j % 2, 2 * g + j // 2)

                for_groups(dve, HEADS // 4, head_group, peel_first=True)

                def residual_unit(u, n, next_tiles, dst, count, other=None):
                    read_out(u)
                    if other is not None and n == 0:
                        split(other, FULL)
                    if next_tiles:
                        split(Unit(u.n + 2, (u.slot + 2) % SLOTS, 0), next_tiles)
                    feed(n, dst, count)

                for a in range(3):
                    split(unit(base + O_BASE, SLOTS, 0, a + 2), FULL)
                    attention(a, HEADS)
                if layer == 0:
                    attention(0, HEADS + 1)
                    attention(1, HEADS + 1)
                for n in range(4):
                    residual_unit(unit(base + O_BASE, SLOTS, 0, n), n, 0, feeds(layer, "o"), X_HEADS[layer] + n,
                                  unit(base + O_BASE, SLOTS, 1, 1))
                with dve.Fori(1, XT // SLOTS) as g:
                    for j in range(SLOTS):
                        residual_unit(unit(base + O_BASE, SLOTS, g, j), SLOTS * g + j, FULL, feeds(layer, "o"),
                                      X_HEADS[layer] + SLOTS * g + j)

                for c, tiles in enumerate(CHUNKS):
                    last_chunk = c == len(CHUNKS) - 1
                    n_groups = 2 * tiles // SLOTS
                    pairs = layer * sum(CHUNKS) + sum(CHUNKS[:c])
                    x_before = X_ACT[layer][c] - tiles

                    def gu_group(g):
                        for j in range(SLOTS):
                            read_out(unit(base + GU_BASE[c], SLOTS, g, j))
                            split(unit(base + GU_BASE[c], SLOTS, g, j + 2),
                                  SHORT if last_chunk and last_two(g, n_groups, j) else FULL)
                            pair = 2 * g + j // 2
                            if j % 2 == 1:
                                hi, lo = x_tile(xc, pair)
                                dve.wait_ge(x_hi, x_before + pair + 1)
                                v.tensor_tensor(lo, hidden[:, :], hi.bitcast(F32), ALU.subtract).then_inc(x_lo, 1)

                    for_groups(dve, n_groups, gu_group, peel_last=last_chunk)
                    n_down = XT // SLOTS
                    dst = feeds(layer, "down") if last_chunk else []

                    def down_group(g):
                        for j in range(SLOTS):
                            if not last_chunk:
                                nxt = FULL
                            elif last_two(g, n_down, j):
                                nxt = 0 if layer == DEPTH - 1 else FULL
                            else:
                                nxt = SHORT
                            n = SLOTS * g + j
                            residual_unit(unit(base + DOWN_BASE[c], SLOTS, g, j), n, nxt, dst,
                                          X_ACT[layer][c] + 2 * n)

                    for_groups(dve, n_down, down_group, peel_last=last_chunk)

            dve.wait_ge(rs_ready, 5)
            for t in range(XT):
                v.scalar_tensor_tensor(h[:, t, :], h[:, t, :], gain[:, G_FINAL + t:G_FINAL + t + 1], rs[:, :],
                                       ALU.mult, ALU.mult).then_inc(y_made, 1)

        @block.gpsimd
        def _(pool):
            p = nc.gpsimd
            p.memset(ident[:, :], 0.0).then_inc(pool_chain, 1)
            p.memset(ones[:, :], 1.0)
            p.memset(neg_ones[:, :], -1.0).then_inc(pool_chain, 1)
            p.memset(eps[:, :], EPS)
            pool.wait_ge(pool_chain, 2)
            p.affine_select(out=ident[:, :], in_=ident[:, :], compare_op=ALU.not_equal, fill=1.0, base=0,
                            pattern=[[-1, P]], channel_multiplier=1)
            p.affine_select(out=neg_tri[:, :], in_=neg_ones[:, :], compare_op=ALU.is_ge, fill=0.0, base=0,
                            pattern=[[-1, P]], channel_multiplier=1).then_inc(consts_made, 1)
            p.memset(ssq[:, :], 0.0).then_inc(ssq_zeroed, 1)
            pool.wait_ge(ssq_zeroed, 1)

            def add_square(count):
                pool.wait_ge(sq_ready, count)
                wait(pool, ssq_added, count - 1)
                p.tensor_tensor(ssq[:, :], ssq[:, :], sq[:, :], ALU.add).then_inc(ssq_added, 1)

            def clear_squares(norm):
                pool.wait_ge(norm_full, norm + 1)
                p.memset(ssq[:, :], 0.0).then_inc(ssq_zeroed, 1)
                pool.wait_ge(ssq_zeroed, norm + 2)

            for t in range(XT):
                add_square(t + 1)

            def attention0(r, i):
                prev2 = not isinstance(i, int) or i >= 2
                if r == 0 and prev2:
                    pool.wait_ge(o_rs_ready, i - 1)
                    p.tensor_tensor(o_rs[:, :], o_raw[:, :], o_rs[:, :], ALU.mult).then_inc(o_normed, 1)

            def diagonals(buf):
                stand_alone(pool)
                d = buf.rearrange("p (a b) -> p a b", a=3)[:, 0:3:2, :]
                return p.affine_select(out=d, in_=d, compare_op=ALU.is_gt, fill=0.0, base=0,
                                       pattern=[[0, 2], [1, P]], channel_multiplier=-1)

            def attention1(r, i):
                new = not isinstance(i, int) or i < HEADS
                prev = not isinstance(i, int) or 1 <= i <= HEADS
                if r == 0 and prev:
                    pool.wait_ge(stick_exp, i)
                    diagonals(a_t[:, :]).then_inc(stick_masked, 1)
                elif r == 2 and new:
                    pool.wait_ge(sp_ready, i + 1)
                    diagonals(sc[:, 0, :]).then_inc(sp_masked, 1)

            for layer in range(DEPTH):
                base = layer * UNITS_PER_LAYER
                attention = attention0 if layer == 0 else attention1

                def head_group(g):
                    for j in range(4):
                        i = 4 * g + j
                        for r in range(3):
                            u = unit(base, 12, g, 3 * j + r)
                            if isinstance(g, int) and j == 0 and r == 0:
                                clear_squares(2 * layer)
                                pool.wait_ge(rs_ready, 2 * layer + 1)
                            pool.wait_ge(summed, u.n + 1)
                            if r == 2:
                                wait(pool, v_turned, HEADS * layer + i)
                            else:
                                wait(pool, scores_full, 2 * i if layer == 0 else 2 * HEADS + i)
                            p.tensor_tensor((q_t, k_t, v_t)[r][:, :], total[:, u.slot % 2, :],
                                            (rs_q if r == 0 else rs)[:, :], ALU.mult).then_inc(took, 1)
                            attention(r, i)

                for_groups(pool, HEADS // 4, head_group, peel_first=True)
                for r in range(3):
                    attention(r, HEADS)
                if layer == 0:
                    attention(0, HEADS + 1)

                def residual_unit(u, n, count):
                    pool.wait_ge(summed, u.n + 1)
                    p.tensor_tensor(h_tile(n), h_tile(n), total[:, u.slot % 2, :], ALU.add).then_inc(took, 1)
                    if count is not None:
                        add_square(count)

                def o_group(g):
                    for j in range(SLOTS):
                        n = SLOTS * g + j
                        residual_unit(unit(base + O_BASE, SLOTS, g, j), n, XT * (2 * layer + 1) + n + 1)

                for_groups(pool, XT // SLOTS, o_group)
                for c, tiles in enumerate(CHUNKS):
                    pairs = layer * sum(CHUNKS) + sum(CHUNKS[:c])

                    def gu_group(g):
                        for j in range(SLOTS):
                            u = unit(base + GU_BASE[c], SLOTS, g, j)
                            if c == 0 and isinstance(g, int) and j == 0:
                                clear_squares(2 * layer + 1)
                                pool.wait_ge(rs_ready, 2 * layer + 2)
                            pair = 2 * g + j // 2
                            pool.wait_ge(summed, u.n + 1)
                            if j % 2 == 0:
                                p.tensor_tensor(gate[:, :], total[:, u.slot % 2, :], rs[:, :], ALU.mult)\
                                 .then_inc(took, 1)
                                pool.wait_ge(silu_ready, pairs + pair + 1)
                                p.tensor_tensor(gate_w[:, :], gate_silu[:, :], rs[:, :], ALU.mult)\
                                 .then_inc(w_ready, 1)
                            else:
                                pool.wait_ge(w_ready, pairs + pair + 1)
                                pool.wait_ge(x_lo, X_ACT[layer][c] - tiles + pair)
                                p.tensor_tensor(hidden[:, :], total[:, u.slot % 2, :], gate_w[:, :], ALU.mult)\
                                 .then_inc(took, 1)

                    for_groups(pool, 2 * tiles // SLOTS, gu_group, peel_first=c == 0)

                    def down_group(g):
                        for j in range(SLOTS):
                            n = SLOTS * g + j
                            residual_unit(unit(base + DOWN_BASE[c], SLOTS, g, j), n,
                                          XT * (2 * layer + 2) + n + 1 if c == len(CHUNKS) - 1 else None)

                    for_groups(pool, XT // SLOTS, down_group)


def bucket_rows_by_shape():
    rows = np.zeros((N_BUCKETS + 1, 3 * P), np.float32)
    exact = N_BUCKETS // 2
    n = np.arange(3 * P - (P - 1))
    nf = np.maximum(n, 1).astype(np.float32)
    large = exact + (np.log(nf / np.float32(exact)) / np.float32(np.log(MAX_DISTANCE / exact))
                     * np.float32(N_BUCKETS - exact)).astype(np.int32)
    bucket = np.where(n < exact, n, np.minimum(large, N_BUCKETS - 1))
    rows[bucket, n + P - 1] = 1.0
    rows[N_BUCKETS, 0:P - 1] = 1.0
    return rows


def weight_units(inputs):
    def cols(w):
        k, n = w.shape
        return w.reshape(k // P, P, n // P, P).transpose(2, 1, 0, 3)

    full = np.empty((DEPTH * FULL_PER_LAYER, P, FULL * P), np.float32)
    short = np.empty((DEPTH * XT, P, SHORT * P), np.float32)
    for layer in range(DEPTH):
        at = layer * FULL_PER_LAYER
        view = full[at:at + FULL_PER_LAYER].reshape(FULL_PER_LAYER, P, FULL, P)
        if layer == 0:
            qkv = cols(np.asarray(inputs["diff_w_qkv"])[0])
            parts = [qkv[0:HEADS], qkv[HEADS:2 * HEADS], qkv[2 * HEADS:]]
            w_o = np.asarray(inputs["diff_w_o"])[0]
        else:
            kv = cols(np.asarray(inputs["sb_w_kv"]))
            parts = [cols(np.asarray(inputs["sb_w_q"])[0]), kv[0:HEADS], kv[HEADS:]]
            w_o = np.asarray(inputs["sb_w_o"])[0]
        for r in range(3):
            view[r:HEAD_UNITS:3] = parts[r]
        w_o = cols(w_o)
        view[O_BASE:O_BASE + 4] = w_o[0:4].reshape(4, P, 4, 4, P).transpose(2, 1, 3, 0, 4).reshape(4, P, FULL, P)
        view[O_BASE + 4:O_BASE + XT] = w_o[4:]
        w_gate = cols(np.asarray(inputs["ffn_w_gate"])[layer])
        w_up = cols(np.asarray(inputs["ffn_w_up"])[layer])
        w_down = cols(np.asarray(inputs["ffn_w_down"])[layer])
        f = 0
        for c, tiles in enumerate(CHUNKS):
            view[GU_BASE[c]:DOWN_BASE[c]:2] = w_gate[f:f + tiles]
            view[GU_BASE[c] + 1:DOWN_BASE[c]:2] = w_up[f:f + tiles]
            chunk = w_down[:, :, f:f + tiles, :]
            if tiles == FULL:
                view[DOWN_BASE[c]:DOWN_BASE[c] + XT] = chunk
            else:
                short[layer * XT:(layer + 1) * XT] = chunk.reshape(XT, P, SHORT * P)
            f += tiles
    return full, short


def kernel(**inputs):
    import concourse.bacc as bacc
    from concourse.bass_utils import run_bass_kernel_spmd

    inputs = {k: np.asarray(v) for k, v in inputs.items()}
    full, short = weight_units(inputs)

    def tiles_of(g):
        return g.reshape(XT, P).T

    gains = np.concatenate([tiles_of(inputs["attn_norm_g"][0]), tiles_of(inputs["attn_norm_g"][1]),
                            tiles_of(inputs["ffn_norm_g"][0]), tiles_of(inputs["ffn_norm_g"][1]),
                            tiles_of(inputs["kv_norm_g"]), tiles_of(inputs["final_norm_g"]),
                            inputs["diff_subln_g"][0].reshape(P, 1)], axis=1)
    lambdas = np.stack([inputs["diff_lambda_q1"][0], inputs["diff_lambda_k1"][0],
                        inputs["diff_lambda_q2"][0], inputs["diff_lambda_k2"][0]])
    arrays = {
        "w_full": full, "w_short": short, "x_in": inputs["x"].reshape(S, D), "gains": gains,
        "lambdas": lambdas, "rel_bias": inputs["rel_bias"], "bucket_rows": bucket_rows_by_shape(),
    }
    arrays = {k: np.ascontiguousarray(v) for k, v in arrays.items()}
    nc = bacc.Bacc("TRN2", target_bir_lowering=False, num_devices=1)
    aps = {k: nc.dram_tensor(k, v.shape, F32, kind="ExternalInput").ap() for k, v in arrays.items()}
    bias_rows = nc.dram_tensor("bias_rows", (HEADS, 3 * P), F32, kind="Internal").ap()
    out = nc.dram_tensor("out", (S, D), F32, kind="ExternalOutput").ap()
    trunk(nc, aps["w_full"], aps["w_short"], aps["x_in"], aps["gains"], aps["lambdas"], aps["rel_bias"],
          aps["bucket_rows"], bias_rows, out)
    r = run_bass_kernel_spmd(nc, [arrays], core_ids=[0])
    return r.results[0]["out"].reshape(1, S, D)
```

```python
from collections import namedtuple
from contextlib import ExitStack

import numpy as np

import concourse.bass as bass
from concourse import mybir

F32 = mybir.dt.float32
F32R = mybir.dt.float32r
ALU = mybir.AluOpType
ACT = mybir.ActivationFunctionType

P = 128
D = 2048
S = 256
DEPTH = 2
HEADS = 16
HALF_DIM = 64
D_FF = 5632
EPS = 1e-5
LAMBDA_INIT = 0.2
N_BUCKETS, MAX_DISTANCE = 32, 128
MASKED = -1e30
LN_EXP = "natural_log_exp_and_others"

XT = D // P
CHUNKS = (16, 16, 12)
assert sum(CHUNKS) * P == D_FF
FULL, SHORT = 16, 12

HEAD_UNITS = 3 * HEADS
O_BASE = HEAD_UNITS
FFN_BASE = O_BASE + XT
GU_BASE, DOWN_BASE = [], []
_u = FFN_BASE
for _c in CHUNKS:
    GU_BASE.append(_u)
    DOWN_BASE.append(_u + 2 * _c)
    _u += 2 * _c + XT
UNITS_PER_LAYER = _u
FULL_PER_LAYER = UNITS_PER_LAYER - XT
SLOTS = 4
TOK = S // P

Unit = namedtuple("Unit", "n slot lap")


def unit(base, per_group, g, off):
    return Unit(base + per_group * g + off, off % SLOTS,
                base // SLOTS + per_group // SLOTS * g + off // SLOTS)


def wait(eng, sem, value):
    if not (isinstance(value, int) and value <= 0):
        eng.wait_ge(sem, value)


def stand_alone(eng):
    eng.nop(nofuse=True)


def for_groups(eng, n, body, peel_first=False, peel_last=False):
    lo, hi = (1 if peel_first else 0), (n - 1 if peel_last else n)
    if peel_first:
        body(0)
    if hi > lo:
        with eng.Fori(lo, hi) as g:
            body(g)
    if peel_last:
        body(n - 1)


def last_two(g, n_groups, j):
    return isinstance(g, int) and g == n_groups - 1 and j >= SLOTS - 2


X_START = XT
X_HEADS = [0, 0]
X_O = [0, 0]
X_ACT = [[0] * 3, [0] * 3]
_x = X_START
for _l in range(DEPTH):
    _x += HEADS
    X_HEADS[_l] = _x
    _x += XT
    X_O[_l] = _x
    for _i, _c in enumerate(CHUNKS):
        _x += _c
        X_ACT[_l][_i] = _x
    if _l == 0:
        _x += 2 * XT
X_DOWN0 = X_ACT[0][2] + 2 * XT
KEEP = (0, 4, 1, 2, 6, 5, 3, 7)
NORM_AFTER = (1, 0)
NORM_STEPS = 3
G_ATTN, G_FFN, G_KV, G_FINAL, G_SUBLN = (0, 16), (32, 48), 64, 80, 96
N_GAINS = 97


def trunk(nc, w_full, w_short, x, gains, lambdas, rel_bias, bucket_rows, bias_rows, out):
    ctx = ExitStack()
    with ctx:
        def sb(name, shape, dt=F32):
            return ctx.enter_context(nc.sbuf_tensor(name, shape, dt))

        def sem(name):
            return ctx.enter_context(nc.semaphore(name))

        raw = sb("raw", [P, SLOTS, FULL * P])
        w_hi = sb("w_hi", [P, 4, FULL * P // 2], F32R)
        w_lo = sb("w_lo", [P, 4, FULL * P // 2], F32R)
        xa = sb("xa", [P, XT, 2 * S], F32R)
        xb = sb("xb", [P, XT, 2 * S], F32R)
        xc = sb("xc", [P, XT, 2 * S], F32R)
        h = sb("h", [P, XT, S])
        tmp = sb("tmp", [P, 2, S])
        total = sb("total", [P, 2, S])
        rs = sb("rs", [P, S])
        rs_q = sb("rs_q", [P, S])
        mean_sq = sb("mean_sq", [P, S])
        token_sq = sb("token_sq", [P, TOK, 4])
        token_ss = sb("token_ss", [P, TOK])
        token_rs = sb("token_rs", [P, TOK])
        token_mean_sq = sb("token_mean_sq", [P, TOK])
        ssq = sb("ssq", [P, S])
        sq = sb("sq", [P, S])
        ident = sb("ident", [P, P])
        ones = sb("ones", [P, P])
        neg_tri = sb("neg_tri", [P, P], F32R)
        neg_ones = sb("neg_ones", [P, P], F32R)
        sp_hi = sb("sp_hi", [P, 3 * P], F32R)
        sp_lo = sb("sp_lo", [P, 3 * P], F32R)
        gain = sb("gain", [P, N_GAINS])
        gain_sub = sb("gain_sub", [P, 1])
        eps = sb("eps", [P, 1])
        lam_in = sb("lam_in", [P, 4, HALF_DIM])
        lam_s = sb("lam_s", [P, 8])
        bias = sb("bias", [P, 2, S])
        q_t = sb("q_t", [P, S])
        k_t = sb("k_t", [P, S])
        v_t = sb("v_t", [P, S])
        v_tok = sb("v_tok", [P, S])
        sc = sb("sc", [P, 2, 3 * P])
        a_t = sb("a_t", [P, 3 * P])
        small = sb("small", [P, 20])
        o_raw = sb("o_raw", [P, S])
        o_sq = sb("o_sq", [P, S])
        o_rs = sb("o_rs", [P, S])
        o_mean_sq = sb("o_mean_sq", [P, S])
        o_norm = sb("o_norm", [P, S])
        o_sq_hi, o_sq_lo = sp_hi[:, 0:S], sp_lo[:, 0:S]
        gate = q_t
        gate_silu = k_t
        gate_w = o_raw
        hidden = o_sq
        rel_ext = sc[0:N_BUCKETS + 1, 0, 0:HEADS]
        onehot = sc[0:N_BUCKETS + 1, 1, 0:3 * P]
        rows_sb = a_t[0:HEADS, :]

        bank = [ctx.enter_context(nc.psum_tensor(f"bank{i}", [P, 512], F32)) for i in range(SLOTS)]
        ps_s = [ctx.enter_context(nc.psum_tensor(f"ps_s{i}", [P, 512], F32)) for i in range(2)]
        ps_x = ctx.enter_context(nc.psum_tensor("ps_x", [P, 512], F32))
        ps_y = ctx.enter_context(nc.psum_tensor("ps_y", [P, 512], F32))
        all_banks = [bank[0], bank[2], ps_x, ps_s[0], bank[1], bank[3], ps_y, ps_s[1]]
        x_tok = h[:, :, :].rearrange("p a s -> p (a s)").rearrange("p (t d) -> p t d", t=TOK)

        landed = [sem(f"landed{i}") for i in range(SLOTS)]
        x_landed = [sem(f"x_landed{i}") for i in range(4)]
        consts_landed = sem("consts_landed")
        rows_landed = sem("rows_landed")
        rows_stored = sem("rows_stored")
        bias_landed = [sem(f"bias_landed{i}") for i in range(2)]
        out_stored = sem("out_stored")
        eps_made = sem("eps_made")
        consts_made = sem("consts_made")
        rel_made = sem("rel_made")
        rows_full = sem("rows_full")
        rows_copied = sem("rows_copied")
        turned_in = sem("turned_in")
        h_made = sem("h_made")
        token_squared = sem("token_squared")
        token_summed = sem("token_summed")
        ssq_placed = sem("ssq_placed")
        hi_ready = sem("hi_ready")
        lo_ready = sem("lo_ready")
        used = sem("used")
        first_full = sem("first_full")
        tmp_ready = sem("tmp_ready")
        summed = sem("summed")
        took = sem("took")
        x_hi = sem("x_hi")
        x_lo = sem("x_lo")
        sq_ready = sem("sq_ready")
        ssq_added = sem("ssq_added")
        ssq_zeroed = sem("ssq_zeroed")
        norm_full = sem("norm_full")
        norm_ln = sem("norm_ln")
        rs_rough = sem("rs_rough")
        norm_chain = sem("norm_chain")
        rs_refined = sem("rs_refined")
        rs_ready = sem("rs_ready")
        scores_full = sem("scores_full")
        max_ready = sem("max_ready")
        exp_ready = sem("exp_ready")
        dve_chain = sem("dve_chain")
        bias_chain = sem("bias_chain")
        a_ready = sem("a_ready")
        a_turned = sem("a_turned")
        a_copied = sem("a_copied")
        v_turned = sem("v_turned")
        v_copied = sem("v_copied")
        o_full = sem("o_full")
        o_copied = sem("o_copied")
        o_squared = sem("o_squared")
        o_sq_lo_ready = sem("o_sq_lo_ready")
        o_ss = sem("o_ss")
        o_ln = sem("o_ln")
        o_mean = sem("o_mean")
        o_rs_ready = sem("o_rs_ready")
        o_chain = sem("o_chain")
        o_refined = sem("o_refined")
        o_normed = sem("o_normed")
        lam_sums = sem("lam_sums")
        lam_exps = sem("lam_exps")
        lam_made = sem("lam_made")
        sub_made = sem("sub_made")
        sp_parts = sem("sp_parts")
        sp_ready = sem("sp_ready")
        sp_masked = sem("sp_masked")
        sp_hi_ready = sem("sp_hi_ready")
        sp_lo_ready = sem("sp_lo_ready")
        cum_full = sem("cum_full")
        stick_exp = sem("stick_exp")
        stick_masked = sem("stick_masked")
        silu_ready = sem("silu_ready")
        pool_chain = sem("pool_chain")
        w_ready = sem("w_ready")
        y_made = sem("y_made")
        y_turned = sem("y_turned")
        y_scaled = [sem(f"y_scaled{k}") for k in range(TOK)]

        def half(u, s):
            return (2 * u.slot + s) % 4

        def x_tile(buf, t):
            if isinstance(t, int):
                return buf[:, t, 0:S], buf[:, t, S:2 * S]
            return (buf[:, bass.ds(t, 1), 0:S].rearrange("p a s -> p (a s)"),
                    buf[:, bass.ds(t, 1), S:2 * S].rearrange("p a s -> p (a s)"))

        def h_tile(t):
            return h[:, t, :] if isinstance(t, int) else h[:, bass.ds(t, 1), :].rearrange("p a s -> p (a s)")

        out_banks = [bank, ps_s + [ps_x, ps_y]]

        def g_col(base, t):
            return gain[:, base + t:base + t + 1] if isinstance(t, int) else gain[:, bass.ds(base + t, 1)]

        def feeds(layer, section):
            if section == "o":
                return [(xa, G_FFN[layer])]
            return [(xa, G_ATTN[1]), (xb, G_KV)] if layer == 0 else []

        block = ctx.enter_context(nc.Block())

        @block.sync
        def _(sp):
            x_fourth = D // 4
            for c in range(4):
                cols = slice(c * x_fourth, (c + 1) * x_fourth)
                sp.dma_start(x_tok[:, :, cols], x[:, cols].rearrange("(t p) d -> p t d", p=P))\
                  .then_inc(x_landed[c], 16)
                if c == 0:
                    sp.dma_start(gain[:, :], gains).then_inc(consts_landed, 16)
                    sp.dma_start(lam_in[:, :, :], lambdas.partition_broadcast(P)).then_inc(consts_landed, 16)
                if c == 1:
                    sp.dma_start(raw[:, 0, :], w_full[0]).then_inc(landed[0], 16)
            sp.dma_start(sc[0:N_BUCKETS, 0, 0:HEADS], rel_bias).then_inc(rows_landed, 16)
            sp.dma_start(onehot, bucket_rows).then_inc(rows_landed, 16)

            def load(u, row, src):
                wait(sp, lo_ready, 2 * (u.n - SLOTS) + 2)
                width = FULL * P if src is w_full else SHORT * P
                sp.dma_start(raw[:, u.slot, 0:width], src[row]).then_inc(landed[u.slot], 16)

            def load_bias(head, b):
                wait(sp, max_ready, 2 * (head - 1))
                rows = bass.AP(tensor=bias_rows.tensor, offset=head * 3 * P, ap=[[1, P], [1, S]])
                sp.dma_start(bias[:, b, :], rows).then_inc(bias_landed[b], 16)

            def head_group(g):
                for j in range(4):
                    for r in range(3):
                        u = unit(0, 12, g, 3 * j + r)
                        if not (isinstance(g, int) and u.n == 0):
                            load(u, u.n, w_full)
                    if isinstance(g, int) and j == 0:
                        continue
                    if isinstance(g, int) and j == 1:
                        sp.wait_ge(rows_copied, 1)
                        sp.dma_start(bias_rows, rows_sb).then_inc(rows_stored, 16)
                        sp.wait_ge(rows_stored, 16)
                        load_bias(0, 0)
                    load_bias(4 * g + j, j % 2)

            for_groups(sp, HEADS // 4, head_group, peel_first=True)
            for layer in range(DEPTH):
                base = layer * UNITS_PER_LAYER
                first = HEAD_UNITS if layer == 0 else 0

                def group(g, base=base + first, row=layer * FULL_PER_LAYER + first):
                    for j in range(SLOTS):
                        load(unit(base, SLOTS, g, j), row + SLOTS * g + j, w_full)

                def short_group(g, base=base + FULL_PER_LAYER, row=layer * XT):
                    for j in range(SLOTS):
                        load(unit(base, SLOTS, g, j), row + SLOTS * g + j, w_short)

                for_groups(sp, (FULL_PER_LAYER - first) // SLOTS, group)
                for_groups(sp, XT // SLOTS, short_group)
            for b in range(4):
                for t in range(TOK):
                    sp.wait_ge(y_scaled[t], b + 1)
                    sp.dma_start(out[t * P:(t + 1) * P, b * 512:(b + 1) * 512],
                                 raw[:, t, b * 512:(b + 1) * 512]).then_inc(out_stored, 16)
            sp.wait_ge(out_stored, 16 * 4 * TOK)

        @block.tensor
        def _(pe):
            mm = nc.tensor.matmul

            def tile_products(b, u, i, kt, x_buf, n_half, first, last):
                s, o = i // n_half, i % n_half * P
                k = half(u, s)
                mm(bank[b][:, :], w_hi[:, k, o:o + P], x_buf[:, kt, :], start=first, stop=False)
                return mm(bank[b][:, 0:S], w_lo[:, k, o:o + P], x_buf[:, kt, 0:S], start=False, stop=last)

            def products(u, x_buf, n_tiles, x_count, per_tile=0):
                pe_half = n_tiles // 2
                if isinstance(u.n, int) and u.n < SLOTS:
                    pe.wait_ge(h_made, kept(bank[u.slot]))
                else:
                    wait(pe, summed, u.n - SLOTS + 1)
                for kt in range(n_tiles):
                    if kt % pe_half == 0:
                        wait(pe, lo_ready, 2 * u.n + kt // pe_half + 1)
                    if per_tile:
                        pe.wait_ge(x_lo, x_count - per_tile * (n_tiles - 1 - kt))
                    elif kt == 0:
                        pe.wait_ge(x_lo, x_count - 1)
                    elif kt == n_tiles - 1:
                        pe.wait_ge(x_lo, x_count)
                    last = tile_products(u.slot, u, kt, kt, x_buf, pe_half, kt == 0, kt == n_tiles - 1)
                    if kt % pe_half == pe_half - 1:
                        last.then_inc(used, 1)

            def kept(b):
                return KEEP.index(all_banks.index(b)) + 1

            def norm_sum(n):
                if n == 0:
                    pe.wait_ge(ssq_placed, TOK)
                    pe.wait_ge(h_made, kept(ps_x))
                else:
                    pe.wait_ge(ssq_added, XT * n)
                wait(pe, o_mean, HEADS if n >= 1 else 0)
                wait(pe, rs_ready, n)
                mm(ps_x[:, 0:S], ones[:, :], ssq[:, :], start=True, stop=True).then_inc(norm_full, 1)

            def turn_v(i, layer):
                n = HEADS * layer + i
                pe.wait_ge(took, UNITS_PER_LAYER * layer + 3 * i + 3)
                if layer == 0:
                    wait(pe, o_copied, i)
                else:
                    wait(pe, x_lo, X_DOWN0 + i)
                for t in range(TOK):
                    last = nc.tensor.transpose(ps_y[:, t * P:(t + 1) * P], v_t[:, t * P:(t + 1) * P], ident[:, :])
                last.then_inc(v_turned, 1)

            def weigh_v(i, layer):
                n = HEADS * layer + i
                pe.wait_ge(v_copied, n + 1)
                if layer == 0:
                    pe.wait_ge(a_copied, i + 1)
                else:
                    pe.wait_ge(stick_masked, i + 1)
                mm(ps_y[:, 0:S], v_tok[:, 0:P], a_t[:, 0:S], start=True, stop=False)
                mm(ps_y[:, P:S], v_tok[:, P:2 * P], a_t[:, S:S + P], start=False, stop=True).then_inc(o_full, 1)

            def attention0(r, i):
                new = not isinstance(i, int) or i < HEADS
                prev = not isinstance(i, int) or 1 <= i <= HEADS
                prev2 = not isinstance(i, int) or i >= 2
                if r == 0:
                    if prev:
                        turn_v(i - 1, 0)
                    if prev2:
                        pe.wait_ge(o_sq_lo_ready, i - 1)
                        wait(pe, a_copied, i - 1)
                        mm(ps_x[:, 0:S], neg_ones[:, :], o_sq_hi, start=True, stop=False)
                        mm(ps_x[:, 0:S], neg_ones[:, :], o_sq_lo, start=False, stop=True).then_inc(o_ss, 1)
                elif r == 1 and prev:
                    pe.wait_ge(a_ready, i)
                    wait(pe, o_mean, i - 1)
                    wait(pe, rs_ready, 1)
                    for b in range(3):
                        last = nc.tensor.transpose(ps_x[:, b * P:(b + 1) * P], sc[:, 0, b * P:(b + 1) * P], ident[:, :])
                    last.then_inc(a_turned, 1)
                elif r == 2:
                    if prev:
                        weigh_v(i - 1, 0)
                    if new:
                        pe.wait_ge(took, 3 * i + 2)
                        if isinstance(i, int) and i == 0:
                            pe.wait_ge(h_made, len(KEEP))
                        wait(pe, max_ready, 2 * i)
                        maps = [slice(m * HALF_DIM, (m + 1) * HALF_DIM) for m in range(2)]
                        for m, rows in enumerate(maps):
                            mm(ps_s[m][:, 0:P], q_t[rows, 0:P], k_t[rows, 0:P], start=True, stop=True)
                        for m, rows in enumerate(maps):
                            last = mm(ps_s[m][:, P:3 * P], q_t[rows, P:S], k_t[rows, :], start=True, stop=True,
                                      skip_group_check=True)
                        last.then_inc(scores_full, 1)

            def attention1(r, i):
                new = not isinstance(i, int) or i < HEADS
                prev = not isinstance(i, int) or 1 <= i <= HEADS
                if r == 0 and prev:
                    turn_v(i - 1, 1)
                elif r == 1 and prev:
                    pe.wait_ge(sp_lo_ready, i)
                    for part in (sp_hi, sp_lo):
                        mm(ps_s[0][:, 0:S], neg_tri[:, :], part[:, 0:S], start=False, stop=False,
                           skip_group_check=True)
                        mm(ps_s[0][:, P:S], neg_ones[:, :], part[:, S:3 * P], start=False, stop=False,
                           skip_group_check=True)
                        last = mm(ps_s[0][:, S:3 * P], neg_tri[:, :], part[:, S:3 * P], start=False,
                                  stop=part is sp_lo, skip_group_check=True)
                    last.then_inc(cum_full, 1)
                elif r == 2:
                    if prev:
                        weigh_v(i - 1, 1)
                    if new:
                        pe.wait_ge(took, UNITS_PER_LAYER + 3 * i + 2)
                        wait(pe, stick_exp, i)
                        mm(ps_s[0][:, 0:S], k_t[:, 0:P], q_t[:, :], start=True, stop=True, skip_group_check=True)
                        mm(ps_s[0][:, S:3 * P], k_t[:, P:S], q_t[:, P:S], start=False, stop=True,
                           skip_group_check=True).then_inc(scores_full, 1)

            def o_pieces(kt, layer):
                attention = attention0 if layer == 0 else attention1
                if kt in (3, 7, 9):
                    attention((3, 7, 9).index(kt), HEADS)
                elif kt == 10 and layer == 0:
                    attention(0, HEADS + 1)

            pe.wait_ge(consts_made, 1)
            for t in range(XT):
                if t % 4 == 0:
                    pe.wait_ge(x_landed[t // 4], 16)
                for k in range(TOK):
                    last = nc.tensor.transpose(all_banks[t // 2][:, (t % 2 * TOK + k) * P:(t % 2 * TOK + k + 1) * P],
                                               x_tok[:, k, t * P:(t + 1) * P], ident[:, :])
                if t % 2 == 1:
                    last.then_inc(turned_in, 1)

            for layer in range(DEPTH):
                base = layer * UNITS_PER_LAYER
                attention = attention0 if layer == 0 else attention1

                def head_group(g):
                    for j in range(4):
                        i = 4 * g + j
                        for r in range(3):
                            kv = layer == 1 and r > 0
                            first = isinstance(g, int) and j == 0 and r == 0
                            products(unit(base, 12, g, 3 * j + r), xb if kv else xa, FULL,
                                     X_START if layer == 0 else X_DOWN0, (layer + 1) * first)
                            if isinstance(g, int) and j == 0 and r == NORM_AFTER[layer]:
                                norm_sum(2 * layer)
                                if layer == 0:
                                    pe.wait_ge(rel_made, 1)
                                    pe.wait_ge(rows_landed, 32)
                                    pe.wait_ge(h_made, kept(ps_y))
                                    mm(ps_y[0:HEADS, 0:3 * P], rel_ext, onehot, start=True, stop=True)\
                                        .then_inc(rows_full, 1)
                            attention(r, i)

                for_groups(pe, HEADS // 4, head_group, peel_first=True)

                heads_out = xb if layer == 0 else xc
                for a in range(4):
                    u = unit(base + O_BASE, SLOTS, 0, a)
                    for pair in range(2):
                        pe.wait_ge(lo_ready, 2 * u.n + pair + 1)
                        final = a == 3 and pair == 1
                        order = [(kk, n) for kk in (2 * pair, 2 * pair + 1) for n in range(4)]
                        if final:
                            order.sort(key=lambda kk_n: kk_n[1])
                        for kk, n in order:
                            kt = 4 * a + kk
                            if n == 0:
                                wait(pe, x_lo, X_HEADS[layer] - XT + kt + 1)
                            if kt == 0:
                                pe.wait_ge(summed, u.n + n - SLOTS + 1)
                            last = tile_products(n, u, 4 * kk + n, kt, heads_out, 8, kt == 0, kt == XT - 1)
                            if final and kk == 3 and n < 3:
                                last.then_inc(first_full, 1)
                            if not final and n == 3 and kk % 2 == 0:
                                o_pieces(kt, layer)
                        last.then_inc(used, 1)
                        if not final:
                            o_pieces(kt, layer)

                def o_group(g):
                    for j in range(SLOTS):
                        products(unit(base + O_BASE, SLOTS, g, j), heads_out, FULL, X_HEADS[layer])

                with pe.Fori(1, XT // SLOTS) as g:
                    o_group(g)

                for c, tiles in enumerate(CHUNKS):
                    def gu_group(g):
                        for j in range(SLOTS):
                            first = c == 0 and isinstance(g, int) and j == 0
                            products(unit(base + GU_BASE[c], SLOTS, g, j), xa, FULL, X_O[layer], int(first))
                            if first:
                                norm_sum(2 * layer + 1)

                    def down_group(g):
                        for j in range(SLOTS):
                            products(unit(base + DOWN_BASE[c], SLOTS, g, j), xc, tiles, X_ACT[layer][c])

                    for_groups(pe, 2 * tiles // SLOTS, gu_group, peel_first=c == 0)
                    for_groups(pe, XT // SLOTS, down_group)

            for t in range(XT):
                b = t // 4
                pe.wait_ge(y_made, t + 1)
                if t == 0:
                    pe.wait_ge(summed, DEPTH * UNITS_PER_LAYER - 1)
                elif t == 12:
                    pe.wait_ge(summed, DEPTH * UNITS_PER_LAYER)
                    pe.wait_ge(rs_ready, 5)
                for k in range(TOK):
                    last = nc.tensor.transpose(out_banks[k][b][:, t % 4 * P:(t % 4 + 1) * P],
                                               h[:, t, k * P:(k + 1) * P], ident[:, :])
                if t % 4 == 3:
                    last.then_inc(y_turned, 1)
                if t == 5:
                    pe.wait_ge(ssq_added, XT * 4 - 1)
                    pe.wait_ge(sq_ready, XT * 4)
                    for k in range(TOK):
                        tokens = slice(k * P, (k + 1) * P)
                        mm(ps_y[:, k:k + 1], ssq[:, tokens], ones[:, 0:1], start=True, stop=False,
                           skip_group_check=True)
                        last = mm(ps_y[:, k:k + 1], sq[:, tokens], ones[:, 0:1], start=False, stop=True,
                                  skip_group_check=True)
                    last.then_inc(norm_full, 1)

        @block.scalar
        def _(act):
            f = nc.scalar.activation

            def split(u, tiles):
                w = tiles // 2 * P
                for s in range(2):
                    if s == 0:
                        act.wait_ge(landed[u.slot], 16 * u.lap + 16)
                    wait(act, used, 2 * u.n + s - 3)
                    f(w_hi[:, half(u, s), 0:w], raw[:, u.slot, s * w:(s + 1) * w], ACT.Copy).then_inc(hi_ready, 1)

            def read_out(u, full_sem=used, full=None):
                act.wait_ge(full_sem, 2 * u.n + 2 if full is None else full)
                wait(act, summed, u.n - 1)
                f(tmp[:, u.slot % 2, :], bank[u.slot][:, S:2 * S], ACT.Copy).then_inc(tmp_ready, 1)

            def feed(n, dst, count):
                for d, (buf, g) in enumerate(dst):
                    stand_alone(act)
                    f(x_tile(buf, n)[0], h_tile(n), ACT.Copy, scale=g_col(g, n)).then_inc(x_hi, 1)

            def square(n, done):
                wait(act, ssq_added, done)
                stand_alone(act)
                f(sq[:, :], h_tile(n), ACT.Square).then_inc(sq_ready, 1)

            def norm_scale(n, sums=ps_x[:, 0:S], rs=rs[:, :]):
                act.wait_ge(norm_full, n + 1)
                f(rs, sums, ACT.Ln, bias=eps[:, 0:1], scale=1.0 / D).then_inc(norm_ln, 1)
                act.wait_ge(norm_ln, n + 1)
                f(rs, rs, ACT.Exp, scale=-0.5).then_inc(rs_rough, 1)

            def attention0(r, i):
                new = not isinstance(i, int) or i < HEADS
                prev = not isinstance(i, int) or 1 <= i <= HEADS
                prev2 = not isinstance(i, int) or i >= 2
                if r == 0:
                    if prev:
                        act.wait_ge(v_turned, i)
                        wait(act, o_full, i - 1)
                        f(v_tok[:, :], ps_y[:, 0:S], ACT.Copy).then_inc(v_copied, 1)
                    if prev2:
                        act.wait_ge(o_ss, i - 1)
                        wait(act, o_refined, i - 2)
                        f(o_rs[:, :], ps_x[:, 0:S], ACT.Ln, bias=eps[:, 0:1], scale=-1.0 / P).then_inc(o_ln, 1)
                        act.wait_ge(o_ln, i - 1)
                        f(o_rs[:, :], o_rs[:, :], ACT.Exp, scale=-0.5).then_inc(o_rs_ready, 1)
                        f(o_mean_sq[:, :], ps_x[:, 0:S], ACT.Copy, scale=-1.0 / P).then_inc(o_mean, 1)
                elif r == 1 and prev2:
                    act.wait_ge(o_refined, i - 1)
                    stand_alone(act)
                    f(x_tile(xb, i - 2)[0], o_norm[:, :], ACT.Copy, scale=gain_sub[:, 0:1]).then_inc(x_hi, 1)
                elif r == 2:
                    if prev:
                        act.wait_ge(o_copied, i)
                        wait(act, o_ss, i - 1)
                        f(o_sq_hi, o_raw[:, :], ACT.Square)
                        f(o_sq[:, :], o_raw[:, :], ACT.Square).then_inc(o_squared, 1)
                    if new:
                        for m in range(2):
                            act.wait_ge(max_ready, 2 * i + m + 1)
                            for q, cols in enumerate((slice(0, P), slice(P, 3 * P))):
                                c = 2 * m + q
                                last = f(sc[:, m, cols], sc[:, m, cols], ACT.Exp, bias=small[:, c:c + 1],
                                         accum_out=small[:, 4 + c:5 + c])
                            last.then_inc(exp_ready, 1)

            def attention1(r, i):
                new = not isinstance(i, int) or i < HEADS
                prev = not isinstance(i, int) or 1 <= i <= HEADS
                if r == 0 and prev:
                    act.wait_ge(v_turned, HEADS + i)
                    wait(act, o_full, HEADS + i - 1)
                    f(v_tok[:, :], ps_y[:, 0:S], ACT.Copy).then_inc(v_copied, 1)
                    act.wait_ge(sp_masked, i)
                    f(sp_hi[:, :], sc[:, 0, :], ACT.Copy).then_inc(sp_hi_ready, 1)
                elif r == 1 and prev:
                    act.wait_ge(cum_full, i)
                    f(a_t[:, :], ps_s[0][:, 0:3 * P], ACT.Exp).then_inc(stick_exp, 1)
                elif r == 2:
                    if prev:
                        act.wait_ge(o_full, HEADS + i)
                        stand_alone(act)
                        f(x_tile(xc, i - 1)[0], ps_y[:, 0:S], ACT.Copy).then_inc(x_hi, 1)
                    if new:
                        act.wait_ge(scores_full, HEADS + i + 1)
                        wait(act, cum_full, i)
                        f(sc[:, 1, :], ps_s[0][:, 0:3 * P], ACT.Abs).then_inc(sp_parts, 1)
                        act.wait_ge(sp_parts, 3 * i + 1)
                        f(sc[:, 1, :], sc[:, 1, :], ACT.Exp, scale=-1.0).then_inc(sp_parts, 1)
                        act.wait_ge(sp_parts, 3 * i + 2)
                        f(sc[:, 1, :], sc[:, 1, :], ACT.Ln, bias=1.0).then_inc(sp_parts, 1)

            nc.scalar.preload_act_table_set(LN_EXP)
            act.wait_ge(consts_landed, 32)
            act.wait_ge(lam_sums, 2)
            f(lam_s[:, 2:4], lam_s[:, 0:2], ACT.Exp).then_inc(lam_exps, 1)
            f(gain_sub[:, 0:1], gain[:, G_SUBLN:G_SUBLN + 1], ACT.Copy, scale=1.0 - LAMBDA_INIT).then_inc(sub_made, 1)

            def square_tokens(c):
                act.wait_ge(x_landed[c], 16)
                for k in range(TOK):
                    f(xb[:, 2 * c + k, :], x_tok[:, k, c * 4 * P:(c + 1) * 4 * P], ACT.Square,
                      accum_out=token_sq[:, k, c:c + 1]).then_inc(token_squared, 1)

            act.wait_ge(eps_made, 1)
            for t in range(XT):
                if t == 0:
                    square_tokens(0)
                act.wait_ge(turned_in, t // 2 + 1)
                f(x_tile(xa, t)[0], all_banks[t // 2][:, t % 2 * S:(t % 2 + 1) * S], ACT.Copy,
                  scale=g_col(G_ATTN[0], t)).then_inc(x_hi, 1)
                if t == 7:
                    split(unit(0, SLOTS, 0, 0), FULL)
            split(unit(0, SLOTS, 0, 1), FULL)
            for c in range(1, 4):
                square_tokens(c)

            for layer in range(DEPTH):
                base = layer * UNITS_PER_LAYER
                attention = attention0 if layer == 0 else attention1

                def head_group(g):
                    for j in range(4):
                        for r in range(3):
                            off = 3 * j + r
                            read_out(unit(base, 12, g, off))
                            if isinstance(g, int) and off == NORM_AFTER[layer]:
                                norm_scale(2 * layer)
                            split(unit(base, 12, g, off + 2), FULL)
                            attention(r, 4 * g + j)

                for_groups(act, HEADS // 4, head_group, peel_first=True)

                def finish(u, n, dst, norm):
                    act.wait_ge(took, u.n + 1)
                    feed(n, dst, 0)
                    square(n, XT * (norm - 1) + n)
                    if norm == 2 * DEPTH:
                        act.wait_ge(sq_ready, XT * (norm - 1) + n + 1)
                        stand_alone(act)
                        f(h_tile(n), h_tile(n), ACT.Copy, scale=g_col(G_FINAL, n)).then_inc(y_made, 1)

                def residual_unit(u, n, next_tiles, dst, norm):
                    read_out(u)
                    if next_tiles:
                        split(Unit(u.n + 2, (u.slot + 2) % SLOTS, u.lap + (u.slot + 2) // SLOTS), next_tiles)
                    if norm is not None:
                        finish(u, n, dst, norm)

                split(unit(base + O_BASE, SLOTS, 0, 2), FULL)
                attention(0, HEADS)
                attention(1, HEADS)
                attention(2, HEADS)
                split(unit(base + O_BASE, SLOTS, 0, 3), FULL)
                if layer == 0:
                    attention(0, HEADS + 1)
                    attention(1, HEADS + 1)
                split(unit(base + O_BASE, SLOTS, 1, 0), FULL)
                for n in range(SLOTS + 1):
                    if n < SLOTS - 1:
                        read_out(unit(base + O_BASE, SLOTS, 0, n), first_full, (SLOTS - 1) * layer + n + 1)
                    elif n < SLOTS:
                        read_out(unit(base + O_BASE, SLOTS, 0, n))
                    if n == 0:
                        split(unit(base + O_BASE, SLOTS, 1, 1), FULL)
                    else:
                        finish(unit(base + O_BASE, SLOTS, 0, n - 1), n - 1, feeds(layer, "o"), 2 * layer + 1)
                with act.Fori(1, XT // SLOTS) as g:
                    for j in range(SLOTS):
                        residual_unit(unit(base + O_BASE, SLOTS, g, j), SLOTS * g + j, FULL, feeds(layer, "o"),
                                      2 * layer + 1)

                for c, tiles in enumerate(CHUNKS):
                    last_chunk = c == len(CHUNKS) - 1
                    n_groups = 2 * tiles // SLOTS
                    pairs = base // UNITS_PER_LAYER * sum(CHUNKS) + sum(CHUNKS[:c])

                    def gu_group(g):
                        for j in range(SLOTS):
                            u = unit(base + GU_BASE[c], SLOTS, g, j)
                            read_out(u)
                            if c == 0 and isinstance(g, int) and g == 0 and j == 0:
                                norm_scale(2 * layer + 1)
                            split(unit(base + GU_BASE[c], SLOTS, g, j + 2),
                                  SHORT if last_chunk and last_two(g, n_groups, j) else FULL)
                            act.wait_ge(took, u.n + 1)
                            pair = 2 * g + j // 2
                            if j % 2 == 0:
                                f(gate_silu[:, :], gate[:, :], ACT.Silu).then_inc(silu_ready, 1)
                            else:
                                stand_alone(act)
                                f(x_tile(xc, pair)[0], hidden[:, :], ACT.Copy).then_inc(x_hi, 1)

                    for_groups(act, n_groups, gu_group, peel_first=c == 0, peel_last=last_chunk)
                    norm = 2 * layer + 2 if last_chunk else None
                    if last_chunk:
                        nc.scalar.preload_act_table_set(LN_EXP)
                    n_down = XT // SLOTS

                    def down_group(g):
                        for j in range(SLOTS):
                            if not last_chunk:
                                nxt = FULL
                            elif last_two(g, n_down, j):
                                nxt = 0 if layer == DEPTH - 1 else FULL
                            else:
                                nxt = SHORT
                            residual_unit(unit(base + DOWN_BASE[c], SLOTS, g, j), SLOTS * g + j, nxt,
                                          feeds(layer, "down"), norm)

                    for_groups(act, n_down, down_group, peel_last=last_chunk)

            norm_scale(4, ps_y[:, 0:TOK], token_rs[:, :])
            act.wait_ge(rs_ready, 5)
            for b in range(4):
                act.wait_ge(y_turned, b + 1)
                f(raw[:, 0, b * 512:(b + 1) * 512], out_banks[0][b][:, :], ACT.Copy, scale=token_rs[:, 0:1])\
                 .then_inc(y_scaled[0], 1)

        @block.vector
        def _(dve):
            v = nc.vector

            def split(u, tiles):
                w = tiles // 2 * P
                for s in range(2):
                    dve.wait_ge(hi_ready, 2 * u.n + s + 1)
                    k = half(u, s)
                    v.tensor_tensor(w_lo[:, k, 0:w], raw[:, u.slot, s * w:(s + 1) * w],
                                    w_hi[:, k, 0:w].bitcast(F32), ALU.subtract).then_inc(lo_ready, 1)

            def read_out(u):
                dve.wait_ge(tmp_ready, u.n + 1)
                wait(dve, took, u.n - 1)
                v.tensor_tensor(total[:, u.slot % 2, :], bank[u.slot][:, 0:S], tmp[:, u.slot % 2, :],
                                ALU.add).then_inc(summed, 1)

            def norm_scale(n, q_scale=None, sums=ps_x[:, 0:S], rs=rs[:, :], mean_sq=mean_sq[:, :]):
                steps = NORM_STEPS * n
                dve.wait_ge(norm_ln, n + 1)
                v.tensor_scalar(mean_sq, sums, 1.0 / D, EPS, ALU.mult, ALU.add).then_inc(norm_chain, 1)
                dve.wait_ge(rs_rough, n + 1)
                wait(dve, norm_chain, steps + 1)
                v.scalar_tensor_tensor(mean_sq, mean_sq, -0.5, rs, ALU.mult, ALU.mult)\
                 .then_inc(norm_chain, 1)
                dve.wait_ge(norm_chain, steps + 2)
                v.tensor_tensor(mean_sq, mean_sq, rs, ALU.mult).then_inc(norm_chain, 1)
                dve.wait_ge(norm_chain, steps + 3)
                last = v.scalar_tensor_tensor(rs, mean_sq, 1.5, rs, ALU.add, ALU.mult)
                if q_scale is not None:
                    last.then_inc(rs_refined, 1)
                    dve.wait_ge(rs_refined, n // 2 + 1)
                    last = v.tensor_scalar(rs_q[:, :], rs, q_scale, None, ALU.mult)
                last.then_inc(rs_ready, 1)

            def feed(n, dst, count):
                for d, (buf, g) in enumerate(dst):
                    hi, lo = x_tile(buf, n)
                    dve.wait_ge(x_hi, count + d + 1)
                    v.scalar_tensor_tensor(lo, h_tile(n), g_col(g, n), hi.bitcast(F32),
                                           ALU.mult, ALU.subtract).then_inc(x_lo, 1)

            def attention0(r, i, b=0, lap=0):
                new = not isinstance(i, int) or i < HEADS
                prev = not isinstance(i, int) or 1 <= i <= HEADS
                prev2 = not isinstance(i, int) or i >= 2
                if r == 0 and prev:
                    dve.wait_ge(exp_ready, 2 * i)
                    v.reciprocal(small[:, 8:12], small[:, 4:8]).then_inc(dve_chain, 1)
                    dve.wait_ge(dve_chain, 3 * (i - 1) + 1)
                    v.tensor_scalar(small[:, 12:14], small[:, 10:12], lam_s[:, 5:6], None, ALU.mult)\
                     .then_inc(dve_chain, 1)
                    dve.wait_ge(dve_chain, 3 * (i - 1) + 2)
                    for q, cols in enumerate((slice(0, P), slice(P, 3 * P))):
                        last = v.tensor_scalar(sc[:, 1, cols], sc[:, 1, cols], small[:, 12 + q:13 + q], None, ALU.mult)
                    last.then_inc(dve_chain, 1)
                    dve.wait_ge(dve_chain, 3 * (i - 1) + 3)
                    for q, cols in enumerate((slice(0, P), slice(P, 3 * P))):
                        last = v.scalar_tensor_tensor(sc[:, 0, cols], sc[:, 0, cols], small[:, 8 + q:9 + q],
                                                      sc[:, 1, cols], ALU.mult, ALU.add)
                    last.then_inc(a_ready, 1)
                elif r == 1:
                    if prev:
                        dve.wait_ge(a_turned, i)
                        wait(dve, o_full, i - 1)
                        v.tensor_copy(a_t[:, :], ps_x[:, 0:3 * P]).then_inc(a_copied, 1)
                    if prev2:
                        dve.wait_ge(o_mean, i - 1)
                        v.scalar_tensor_tensor(o_mean_sq[:, :], o_mean_sq[:, :], EPS, o_rs[:, :],
                                               ALU.add, ALU.mult).then_inc(o_chain, 1)
                        dve.wait_ge(o_chain, 2 * i - 3)
                        v.scalar_tensor_tensor(o_mean_sq[:, :], o_mean_sq[:, :], -0.5, o_rs[:, :],
                                               ALU.mult, ALU.mult).then_inc(o_chain, 1)
                        dve.wait_ge(o_chain, 2 * i - 2)
                        dve.wait_ge(o_normed, i - 1)
                        v.scalar_tensor_tensor(o_norm[:, :], o_mean_sq[:, :], 1.5, o_norm[:, :],
                                               ALU.add, ALU.mult).then_inc(o_refined, 1)
                        hi, lo = x_tile(xb, i - 2)
                        dve.wait_ge(o_refined, i - 1)
                        dve.wait_ge(x_hi, X_START + i - 1)
                        v.scalar_tensor_tensor(lo, o_norm[:, :], gain_sub[:, 0:1], hi.bitcast(F32),
                                               ALU.mult, ALU.subtract).then_inc(x_lo, 1)
                elif r == 2:
                    if prev:
                        dve.wait_ge(o_full, i)
                        wait(dve, o_normed, i - 1)
                        v.tensor_copy(o_raw[:, :], ps_y[:, 0:S]).then_inc(o_copied, 1)
                    if new:
                        biased_scores(i, b, lap)
                    if prev:
                        dve.wait_ge(o_squared, i)
                        v.tensor_tensor(o_sq_lo, o_sq[:, :], o_sq_hi.bitcast(F32), ALU.subtract)\
                         .then_inc(o_sq_lo_ready, 1)

            def biased_scores(i, b, lap):
                dve.wait_ge(bias_landed[b], 16 * lap + 16)
                wait(dve, a_turned, i)
                rev = bias[:, b, :]
                rev = bass.AP(tensor=rev.tensor, offset=rev.offset + S - 1, ap=[rev.ap[0], [-1, S]])
                dve.wait_ge(scores_full, i + 1)
                for m in range(2):
                    stand_alone(dve)
                    v.tensor_tensor_reduce(sc[:, m, 0:P], ps_s[m][:, 0:P], rev[:, P:S], 1.0, MASKED,
                                           ALU.add, ALU.max, small[:, 14 + 2 * m:15 + 2 * m])
                    last = v.tensor_tensor_reduce(sc[:, m, P:3 * P], ps_s[m][:, P:3 * P], rev[:, :], 1.0, MASKED,
                                                  ALU.add, ALU.max, small[:, 15 + 2 * m:16 + 2 * m])
                    last.then_inc(bias_chain, 1)
                    dve.wait_ge(bias_chain, 2 * i + m + 1)
                    v.tensor_scalar(small[:, 2 * m:2 * m + 2], small[:, 14 + 2 * m:16 + 2 * m], -1.0, None, ALU.mult)\
                     .then_inc(max_ready, 1)

            def attention1(r, i, b=0, lap=0):
                new = not isinstance(i, int) or i < HEADS
                prev = not isinstance(i, int) or 1 <= i <= HEADS
                if r == 0 and prev:
                    dve.wait_ge(sp_hi_ready, i)
                    v.tensor_tensor(sp_lo[:, :], sc[:, 0, :], sp_hi[:, :].bitcast(F32), ALU.subtract)\
                     .then_inc(sp_lo_ready, 1)
                elif r == 2:
                    if prev:
                        hi, lo = x_tile(xc, i - 1)
                        dve.wait_ge(x_hi, X_DOWN0 + i)
                        v.tensor_tensor(lo, ps_y[:, 0:S], hi.bitcast(F32), ALU.subtract).then_inc(x_lo, 1)
                    if new:
                        dve.wait_ge(sp_parts, 3 * i + 3)
                        v.scalar_tensor_tensor(sc[:, 0, :], ps_s[0][:, 0:3 * P], 0.0, sc[:, 1, :],
                                               ALU.max, ALU.add).then_inc(sp_ready, 1)

            v.memset(sc[N_BUCKETS:N_BUCKETS + 1, 0, 0:HEADS], MASKED).then_inc(rel_made, 1)
            dve.wait_ge(consts_landed, 32)
            for m in range(2):
                v.tensor_tensor_reduce(lam_in[:, 2 * m, :], lam_in[:, 2 * m, :], lam_in[:, 2 * m + 1, :], 1.0, 0.0,
                                       ALU.mult, ALU.add, lam_s[:, m:m + 1]).then_inc(lam_sums, 1)

            def keep_pair(t):
                fourth = t % 4
                dve.wait_ge(turned_in, max(t, 2 * fourth + 1) + 1)
                dve.wait_ge(token_squared, TOK * (fourth + 1))
                v.tensor_copy(h[:, 2 * t:2 * t + 2, :].rearrange("p a s -> p (a s)"), all_banks[t][:, :])\
                 .then_inc(h_made, 1)

            for t in range(XT):
                dve.wait_ge(x_hi, t // 2 * 2 + 2)
                hi, lo = x_tile(xa, t)
                v.scalar_tensor_tensor(lo, all_banks[t // 2][:, t % 2 * S:(t % 2 + 1) * S], g_col(G_ATTN[0], t),
                                       hi.bitcast(F32), ALU.mult, ALU.subtract).then_inc(x_lo, 1)
                if t == 1:
                    keep_pair(0)
                elif t == 7:
                    split(unit(0, SLOTS, 0, 0), FULL)
            keep_pair(KEEP[1])
            split(unit(0, SLOTS, 0, 1), FULL)
            dve.wait_ge(token_squared, 4 * TOK)
            v.tensor_reduce(token_ss[:, :], token_sq[:, :, :], mybir.AxisListType.X, ALU.add).then_inc(token_summed, 1)
            for t in KEEP[2:5]:
                keep_pair(t)

            def rest_of_start():
                for t in KEEP[5:]:
                    keep_pair(t)
                dve.wait_ge(rows_full, 1)
                v.tensor_copy(rows_sb, ps_y[0:HEADS, 0:3 * P]).then_inc(rows_copied, 1)
                dve.wait_ge(lam_exps, 1)
                v.tensor_tensor(lam_s[:, 4:5], lam_s[:, 3:4], lam_s[:, 2:3], ALU.subtract).then_inc(lam_made, 1)
                dve.wait_ge(lam_made, 1)
                v.tensor_scalar(lam_s[:, 5:6], lam_s[:, 4:5], -LAMBDA_INIT, None, ALU.add).then_inc(lam_made, 1)
                dve.wait_ge(lam_made, 2)
                dve.wait_ge(sub_made, 1)

            for layer in range(DEPTH):
                base = layer * UNITS_PER_LAYER
                attention = attention0 if layer == 0 else attention1

                def head_group(g):
                    for j in range(4):
                        for r in range(3):
                            read_out(unit(base, 12, g, 3 * j + r))
                            if isinstance(g, int) and j == 0 and r == NORM_AFTER[layer]:
                                norm_scale(2 * layer, (HALF_DIM if layer == 0 else P) ** -0.5)
                                if layer == 0:
                                    rest_of_start()
                            attention_first = layer == 0 and r == 0
                            if attention_first:
                                attention(r, 4 * g + j, j % 2, 2 * g + j // 2)
                            split(unit(base, 12, g, 3 * j + r + 2), FULL)
                            if not attention_first:
                                attention(r, 4 * g + j, j % 2, 2 * g + j // 2)

                for_groups(dve, HEADS // 4, head_group, peel_first=True)

                def residual_unit(u, n, next_tiles, dst, count):
                    read_out(u)
                    if next_tiles:
                        split(Unit(u.n + 2, (u.slot + 2) % SLOTS, 0), next_tiles)
                    feed(n, dst, count)

                split(unit(base + O_BASE, SLOTS, 0, 2), FULL)
                attention(0, HEADS)
                attention(1, HEADS)
                attention(2, HEADS)
                split(unit(base + O_BASE, SLOTS, 0, 3), FULL)
                if layer == 0:
                    attention(0, HEADS + 1)
                    attention(1, HEADS + 1)
                split(unit(base + O_BASE, SLOTS, 1, 0), FULL)
                for n in range(SLOTS + 1):
                    if n < SLOTS:
                        read_out(unit(base + O_BASE, SLOTS, 0, n))
                    if n == 0:
                        split(unit(base + O_BASE, SLOTS, 1, 1), FULL)
                    else:
                        feed(n - 1, feeds(layer, "o"), X_HEADS[layer] + n - 1)
                with dve.Fori(1, XT // SLOTS) as g:
                    for j in range(SLOTS):
                        residual_unit(unit(base + O_BASE, SLOTS, g, j), SLOTS * g + j, FULL, feeds(layer, "o"),
                                      X_HEADS[layer] + SLOTS * g + j)

                for c, tiles in enumerate(CHUNKS):
                    last_chunk = c == len(CHUNKS) - 1
                    n_groups = 2 * tiles // SLOTS
                    pairs = layer * sum(CHUNKS) + sum(CHUNKS[:c])
                    x_before = X_ACT[layer][c] - tiles

                    def gu_group(g):
                        for j in range(SLOTS):
                            read_out(unit(base + GU_BASE[c], SLOTS, g, j))
                            if c == 0 and isinstance(g, int) and g == 0 and j == 0:
                                norm_scale(2 * layer + 1)
                            split(unit(base + GU_BASE[c], SLOTS, g, j + 2),
                                  SHORT if last_chunk and last_two(g, n_groups, j) else FULL)
                            pair = 2 * g + j // 2
                            if j % 2 == 1:
                                hi, lo = x_tile(xc, pair)
                                dve.wait_ge(x_hi, x_before + pair + 1)
                                v.tensor_tensor(lo, hidden[:, :], hi.bitcast(F32), ALU.subtract).then_inc(x_lo, 1)

                    for_groups(dve, n_groups, gu_group, peel_first=c == 0, peel_last=last_chunk)
                    n_down = XT // SLOTS
                    dst = feeds(layer, "down") if last_chunk else []

                    def down_group(g):
                        for j in range(SLOTS):
                            if not last_chunk:
                                nxt = FULL
                            elif last_two(g, n_down, j):
                                nxt = 0 if layer == DEPTH - 1 else FULL
                            else:
                                nxt = SHORT
                            n = SLOTS * g + j
                            residual_unit(unit(base + DOWN_BASE[c], SLOTS, g, j), n, nxt, dst,
                                          X_ACT[layer][c] + 2 * n)

                    for_groups(dve, n_down, down_group, peel_last=last_chunk)

            norm_scale(4, None, ps_y[:, 0:TOK], token_rs[:, :], token_mean_sq[:, :])
            dve.wait_ge(rs_ready, 5)
            for b in range(4):
                dve.wait_ge(y_turned, b + 1)
                v.tensor_scalar(raw[:, 1, b * 512:(b + 1) * 512], out_banks[1][b][:, :], token_rs[:, 1:2], None,
                                ALU.mult).then_inc(y_scaled[1], 1)

        @block.gpsimd
        def _(pool):
            p = nc.gpsimd
            p.memset(ident[:, :], 0.0).then_inc(pool_chain, 1)
            p.memset(ones[:, :], 1.0)
            p.memset(ssq[:, 0:P], -1.0).then_inc(pool_chain, 1)
            p.memset(eps[:, :], EPS).then_inc(eps_made, 1)
            pool.wait_ge(pool_chain, 2)
            p.affine_select(out=ident[:, :], in_=ident[:, :], compare_op=ALU.not_equal, fill=1.0, base=0,
                            pattern=[[-1, P]], channel_multiplier=1)
            p.affine_select(out=neg_tri[:, :], in_=ssq[:, 0:P], compare_op=ALU.is_ge, fill=0.0, base=0,
                            pattern=[[-1, P]], channel_multiplier=1)
            p.tensor_copy(neg_ones[:, :], ssq[:, 0:P]).then_inc(consts_made, 1)

            def add_square(count):
                pool.wait_ge(sq_ready, count)
                wait(pool, ssq_added, count - 1)
                p.tensor_tensor(ssq[:, :], ssq[:, :], sq[:, :], ALU.add).then_inc(ssq_added, 1)

            def clear_squares(norm):
                pool.wait_ge(norm_full, norm + 1)
                p.memset(ssq[:, :], 0.0).then_inc(ssq_zeroed, 1)
                pool.wait_ge(ssq_zeroed, norm + 1)

            pool.wait_ge(consts_made, 1)
            pool.wait_ge(token_summed, 1)
            for k in range(TOK):
                p.tensor_scalar(ssq[:, k * P:(k + 1) * P], ident[:, :], token_ss[:, k:k + 1], None, ALU.mult)\
                 .then_inc(ssq_placed, 1)

            def attention0(r, i):
                prev2 = not isinstance(i, int) or i >= 2
                if r == 0 and prev2:
                    pool.wait_ge(o_rs_ready, i - 1)
                    wait(pool, x_lo, X_START + i - 2)
                    p.tensor_tensor(o_norm[:, :], o_raw[:, :], o_rs[:, :], ALU.mult).then_inc(o_normed, 1)

            def diagonals(buf):
                stand_alone(pool)
                d = buf.rearrange("p (a b) -> p a b", a=3)[:, 0:3:2, :]
                return p.affine_select(out=d, in_=d, compare_op=ALU.is_gt, fill=0.0, base=0,
                                       pattern=[[0, 2], [1, P]], channel_multiplier=-1)

            def attention1(r, i):
                new = not isinstance(i, int) or i < HEADS
                prev = not isinstance(i, int) or 1 <= i <= HEADS
                if r == 1 and prev:
                    pool.wait_ge(stick_exp, i)
                    diagonals(a_t[:, :]).then_inc(stick_masked, 1)
                elif r == 2 and new:
                    pool.wait_ge(sp_ready, i + 1)
                    diagonals(sc[:, 0, :]).then_inc(sp_masked, 1)

            for layer in range(DEPTH):
                base = layer * UNITS_PER_LAYER
                attention = attention0 if layer == 0 else attention1

                def head_group(g):
                    for j in range(4):
                        i = 4 * g + j
                        for r in range(3):
                            u = unit(base, 12, g, 3 * j + r)
                            if isinstance(g, int) and j == 0 and r == 0:
                                clear_squares(2 * layer)
                                pool.wait_ge(rs_ready, 2 * layer + 1)
                            pool.wait_ge(summed, u.n + 1)
                            if r == 2:
                                wait(pool, v_turned, HEADS * layer + i)
                            else:
                                wait(pool, scores_full, HEADS * layer + i)
                            p.tensor_tensor((q_t, k_t, v_t)[r][:, :], total[:, u.slot % 2, :],
                                            (rs_q if r == 0 else rs)[:, :], ALU.mult).then_inc(took, 1)
                            attention(r, i)

                for_groups(pool, HEADS // 4, head_group, peel_first=True)
                for r in range(3):
                    attention(r, HEADS)
                if layer == 0:
                    attention(0, HEADS + 1)

                def residual_add(u, n):
                    pool.wait_ge(summed, u.n + 1)
                    p.tensor_tensor(h_tile(n), h_tile(n), total[:, u.slot % 2, :], ALU.add).then_inc(took, 1)

                def residual_unit(u, n, count):
                    residual_add(u, n)
                    if count is not None:
                        add_square(count)

                def o_group(g):
                    for j in range(SLOTS):
                        n = SLOTS * g + j
                        residual_unit(unit(base + O_BASE, SLOTS, g, j), n, XT * 2 * layer + n + 1)

                for n in range(SLOTS + 1):
                    if n < SLOTS:
                        residual_add(unit(base + O_BASE, SLOTS, 0, n), n)
                    if n > 0:
                        add_square(XT * 2 * layer + n)
                with pool.Fori(1, XT // SLOTS) as g:
                    o_group(g)
                for c, tiles in enumerate(CHUNKS):
                    pairs = layer * sum(CHUNKS) + sum(CHUNKS[:c])

                    def gu_group(g):
                        for j in range(SLOTS):
                            u = unit(base + GU_BASE[c], SLOTS, g, j)
                            if c == 0 and isinstance(g, int) and j == 0:
                                clear_squares(2 * layer + 1)
                                pool.wait_ge(rs_ready, 2 * layer + 2)
                            pair = 2 * g + j // 2
                            pool.wait_ge(summed, u.n + 1)
                            if j % 2 == 0:
                                p.tensor_tensor(gate[:, :], total[:, u.slot % 2, :], rs[:, :], ALU.mult)\
                                 .then_inc(took, 1)
                                pool.wait_ge(silu_ready, pairs + pair + 1)
                                p.tensor_tensor(gate_w[:, :], gate_silu[:, :], rs[:, :], ALU.mult)\
                                 .then_inc(w_ready, 1)
                            else:
                                pool.wait_ge(w_ready, pairs + pair + 1)
                                pool.wait_ge(x_lo, X_ACT[layer][c] - tiles + pair)
                                p.tensor_tensor(hidden[:, :], total[:, u.slot % 2, :], gate_w[:, :], ALU.mult)\
                                 .then_inc(took, 1)

                    for_groups(pool, 2 * tiles // SLOTS, gu_group, peel_first=c == 0)

                    last_chunk = c == len(CHUNKS) - 1
                    very_last = XT - 1 if last_chunk and layer == DEPTH - 1 else None

                    def down_group(g):
                        for j in range(SLOTS):
                            n = SLOTS * g + j
                            add_it = last_chunk and not (isinstance(n, int) and n == very_last)
                            residual_unit(unit(base + DOWN_BASE[c], SLOTS, g, j), n,
                                          XT * (2 * layer + 1) + n + 1 if add_it else None)

                    for_groups(pool, XT // SLOTS, down_group, peel_last=very_last is not None)


def bucket_rows_by_shape():
    rows = np.zeros((N_BUCKETS + 1, 3 * P), np.float32)
    exact = N_BUCKETS // 2
    n = np.arange(3 * P - (P - 1))
    nf = np.maximum(n, 1).astype(np.float32)
    large = exact + (np.log(nf / np.float32(exact)) / np.float32(np.log(MAX_DISTANCE / exact))
                     * np.float32(N_BUCKETS - exact)).astype(np.int32)
    bucket = np.where(n < exact, n, np.minimum(large, N_BUCKETS - 1))
    rows[bucket, n + P - 1] = 1.0
    rows[N_BUCKETS, 0:P - 1] = 1.0
    return rows


def weight_units(inputs):
    def cols(w):
        k, n = w.shape
        return w.reshape(k // P, P, n // P, P).transpose(2, 1, 0, 3)

    full = np.empty((DEPTH * FULL_PER_LAYER, P, FULL * P), np.float32)
    short = np.empty((DEPTH * XT, P, SHORT * P), np.float32)
    for layer in range(DEPTH):
        at = layer * FULL_PER_LAYER
        view = full[at:at + FULL_PER_LAYER].reshape(FULL_PER_LAYER, P, FULL, P)
        if layer == 0:
            qkv = cols(np.asarray(inputs["diff_w_qkv"])[0])
            parts = [qkv[0:HEADS], qkv[HEADS:2 * HEADS], qkv[2 * HEADS:]]
            w_o = np.asarray(inputs["diff_w_o"])[0]
        else:
            kv = cols(np.asarray(inputs["sb_w_kv"]))
            parts = [cols(np.asarray(inputs["sb_w_q"])[0]), kv[0:HEADS], kv[HEADS:]]
            w_o = np.asarray(inputs["sb_w_o"])[0]
        for r in range(3):
            view[r:HEAD_UNITS:3] = parts[r]
        w_o = cols(w_o)
        view[O_BASE:O_BASE + 4] = w_o[0:4].reshape(4, P, 4, 4, P).transpose(2, 1, 3, 0, 4).reshape(4, P, FULL, P)
        view[O_BASE + 4:O_BASE + XT] = w_o[4:]
        w_gate = cols(np.asarray(inputs["ffn_w_gate"])[layer])
        w_up = cols(np.asarray(inputs["ffn_w_up"])[layer])
        w_down = cols(np.asarray(inputs["ffn_w_down"])[layer])
        f = 0
        for c, tiles in enumerate(CHUNKS):
            view[GU_BASE[c]:DOWN_BASE[c]:2] = w_gate[f:f + tiles]
            view[GU_BASE[c] + 1:DOWN_BASE[c]:2] = w_up[f:f + tiles]
            chunk = w_down[:, :, f:f + tiles, :]
            if tiles == FULL:
                view[DOWN_BASE[c]:DOWN_BASE[c] + XT] = chunk
            else:
                short[layer * XT:(layer + 1) * XT] = chunk.reshape(XT, P, SHORT * P)
            f += tiles
    return full, short


def kernel(**inputs):
    import concourse.bacc as bacc
    from concourse.bass_utils import run_bass_kernel_spmd

    inputs = {k: np.asarray(v) for k, v in inputs.items()}
    full, short = weight_units(inputs)

    def tiles_of(g):
        return g.reshape(XT, P).T

    gains = np.concatenate([tiles_of(inputs["attn_norm_g"][0]), tiles_of(inputs["attn_norm_g"][1]),
                            tiles_of(inputs["ffn_norm_g"][0]), tiles_of(inputs["ffn_norm_g"][1]),
                            tiles_of(inputs["kv_norm_g"]), tiles_of(inputs["final_norm_g"]),
                            inputs["diff_subln_g"][0].reshape(P, 1)], axis=1)
    lambdas = np.stack([inputs["diff_lambda_q1"][0], inputs["diff_lambda_k1"][0],
                        inputs["diff_lambda_q2"][0], inputs["diff_lambda_k2"][0]])
    arrays = {
        "w_full": full, "w_short": short, "x_in": inputs["x"].reshape(S, D), "gains": gains,
        "lambdas": lambdas, "rel_bias": inputs["rel_bias"], "bucket_rows": bucket_rows_by_shape(),
    }
    arrays = {k: np.ascontiguousarray(v) for k, v in arrays.items()}
    nc = bacc.Bacc("TRN2", target_bir_lowering=False, num_devices=1)
    aps = {k: nc.dram_tensor(k, v.shape, F32, kind="ExternalInput").ap() for k, v in arrays.items()}
    bias_rows = nc.dram_tensor("bias_rows", (HEADS, 3 * P), F32, kind="Internal").ap()
    out = nc.dram_tensor("out", (S, D), F32, kind="ExternalOutput").ap()
    trunk(nc, aps["w_full"], aps["w_short"], aps["x_in"], aps["gains"], aps["lambdas"], aps["rel_bias"],
          aps["bucket_rows"], bias_rows, out)
    r = run_bass_kernel_spmd(nc, [arrays], core_ids=[0])
    return r.results[0]["out"].reshape(1, S, D)
```
